# Optimizing a Trainium2 kernel written in Bass

```python
import jax, jax.numpy as jnp
from jax import lax
import numpy as np

D_MODEL = 1024
BATCH = 1
SEQ = 1024
DEPTH = 2

N_MIXERS = 2
N_LAYERS_A = (DEPTH + 1) // 2
N_LAYERS_B = DEPTH // 2
D_FF = 4 * D_MODEL
EPS = 1e-6
CHUNK = 128
A_WIDTH = 2 * D_MODEL
A_GROUPS = 8
A_GROUP_DIM = A_WIDTH // A_GROUPS
B_HEADS = 16
B_HEAD_DIM = D_MODEL // B_HEADS
Q_BLOCK = 128

kernel_name = "hybrid_gmlp_stickbreaking_trunk"

def rms_norm(x, g):
    xf = x.astype(jnp.float32)
    y = xf * lax.rsqrt(jnp.mean(xf * xf, axis=-1, keepdims=True) + EPS)
    return (y * g.astype(jnp.float32)).astype(x.dtype)

def layer_norm(x, g, b):
    xf = x.astype(jnp.float32)
    mu = jnp.mean(xf, axis=-1, keepdims=True)
    xc = xf - mu
    y = xc * lax.rsqrt(jnp.mean(xc * xc, axis=-1, keepdims=True) + EPS)
    return (y * g.astype(jnp.float32) + b.astype(jnp.float32)).astype(x.dtype)

def chunked_gmlp(x, w_in, v_g, v_b, w_s, b_s, w_out):
    bn, s, _ = x.shape
    z = jax.nn.gelu(x @ w_in, approximate=False)
    u, v = jnp.split(z, 2, axis=-1)
    v = layer_norm(v, v_g, v_b)
    nc = s // CHUNK
    v = v.reshape(bn, nc, CHUNK, A_GROUPS, A_GROUP_DIM)
    causal = jnp.tril(jnp.ones((CHUNK, CHUNK), dtype=bool))
    w_causal = jnp.where(causal[None], w_s, jnp.zeros_like(w_s)).astype(v.dtype)
    mixed = jnp.einsum('gts,bcsgd->bctgd', w_causal, v)
    mixed = mixed + b_s.T.astype(v.dtype)[None, None, :, :, None]
    gated = u * mixed.reshape(bn, s, A_WIDTH)
    return gated @ w_out

def stick_breaking_attention(x, w_qkv, w_out):
    bn, s, _ = x.shape
    qkv = (x @ w_qkv).reshape(bn, s, 3, B_HEADS, B_HEAD_DIM)
    q, k, v = qkv[:, :, 0], qkv[:, :, 1], qkv[:, :, 2]
    scale = B_HEAD_DIM ** -0.5
    outs = []
    for blk in range(s // Q_BLOCK):
        q0 = blk * Q_BLOCK
        kv_len = q0 + Q_BLOCK
        qb = q[:, q0:kv_len]
        kb = k[:, :kv_len]
        vb = v[:, :kv_len]
        z = jnp.einsum('bthd,bshd->bhts', qb, kb).astype(jnp.float32) * scale
        t_pos = q0 + jnp.arange(Q_BLOCK)[:, None]
        s_pos = jnp.arange(kv_len)[None, :]
        causal = s_pos < t_pos
        log_keep = jnp.where(causal, jax.nn.log_sigmoid(-z), 0.0)
        survive = lax.cumsum(log_keep, axis=log_keep.ndim - 1, reverse=True) - log_keep
        log_a = jax.nn.log_sigmoid(z) + survive
        a = jnp.where(causal, jnp.exp(log_a), 0.0)
        outs.append(jnp.einsum('bhts,bshd->bthd', a.astype(vb.dtype), vb))
    o = jnp.concatenate(outs, axis=1).reshape(bn, s, D_MODEL)
    return o @ w_out

def squared_relu_mlp(x, w1, w2):
    return jnp.square(jax.nn.relu(x @ w1)) @ w2

def setup_inputs(seed: int = 0) -> dict:
    key = jax.random.key(seed)
    ks = jax.random.split(key, 16)
    f32 = jnp.float32

    def nrm(k, shape, scale):
        return jax.random.normal(k, shape, f32) * scale

    x = jax.random.normal(ks[0], (BATCH, SEQ, D_MODEL), f32)
    norm_mix_pre = 1.0 + nrm(ks[1], (DEPTH, D_MODEL), 0.02)
    norm_mix_post = 1.0 + nrm(ks[2], (DEPTH, D_MODEL), 0.02)
    norm_ffn_pre = 1.0 + nrm(ks[3], (DEPTH, D_MODEL), 0.02)
    norm_ffn_post = 1.0 + nrm(ks[4], (DEPTH, D_MODEL), 0.02)
    a_w_in = nrm(ks[5], (N_LAYERS_A, D_MODEL, 2 * A_WIDTH), D_MODEL ** -0.5)
    a_v_g = 1.0 + nrm(ks[6], (N_LAYERS_A, A_WIDTH), 0.02)
    a_v_b = nrm(ks[7], (N_LAYERS_A, A_WIDTH), 0.02)
    a_w_s = nrm(ks[8], (N_LAYERS_A, A_GROUPS, CHUNK, CHUNK), CHUNK ** -0.5)
    a_b_s = 1.0 + nrm(ks[9], (N_LAYERS_A, A_GROUPS, CHUNK), 0.01)
    a_w_out = nrm(ks[10], (N_LAYERS_A, A_WIDTH, D_MODEL), A_WIDTH ** -0.5)
    b_w_qkv = nrm(ks[11], (N_LAYERS_B, D_MODEL, 3 * D_MODEL), D_MODEL ** -0.5)
    b_w_out = nrm(ks[12], (N_LAYERS_B, D_MODEL, D_MODEL), D_MODEL ** -0.5)
    mlp_w1 = nrm(ks[13], (DEPTH, D_MODEL, D_FF), D_MODEL ** -0.5)
    mlp_w2 = nrm(ks[14], (DEPTH, D_FF, D_MODEL), D_FF ** -0.5)
    return {"x": x, "norm_mix_pre": norm_mix_pre, "norm_mix_post": norm_mix_post,
            "norm_ffn_pre": norm_ffn_pre, "norm_ffn_post": norm_ffn_post,
            "a_w_in": a_w_in, "a_v_g": a_v_g, "a_v_b": a_v_b, "a_w_s": a_w_s,
            "a_b_s": a_b_s, "a_w_out": a_w_out, "b_w_qkv": b_w_qkv, "b_w_out": b_w_out,
            "mlp_w1": mlp_w1, "mlp_w2": mlp_w2}

def reference(x, norm_mix_pre, norm_mix_post, norm_ffn_pre, norm_ffn_post,
              a_w_in, a_v_g, a_v_b, a_w_s, a_b_s, a_w_out,
              b_w_qkv, b_w_out, mlp_w1, mlp_w2):
    for i in range(DEPTH):
        h = rms_norm(x, norm_mix_pre[i])
        j = i // N_MIXERS
        if i % N_MIXERS == 0:
            m = chunked_gmlp(h, a_w_in[j], a_v_g[j], a_v_b[j], a_w_s[j], a_b_s[j], a_w_out[j])
        else:
            m = stick_breaking_attention(h, b_w_qkv[j], b_w_out[j])
        x = x + rms_norm(m, norm_mix_post[i])
        h = rms_norm(x, norm_ffn_pre[i])
        f = squared_relu_mlp(h, mlp_w1[i], mlp_w2[i])
        x = x + rms_norm(f, norm_ffn_post[i])
    return x


_drawn_inputs = setup_inputs


def setup_inputs(seed=0):
    import zlib

    import numpy as np

    out = dict(_drawn_inputs(seed))
    spreads = {}
    factors = {'norm_mix_post': 2.898,
     'norm_ffn_pre': 3.342,
     'norm_ffn_post': 10.38,
     'a_v_g': 33.901,
     'a_v_b': 33.476,
     'a_b_s': 49.698}
    for name, (base, spread) in spreads.items():
        noise = np.random.default_rng([zlib.crc32(name.encode()), seed]).standard_normal(out[name].shape)
        drawn = base * np.exp(spread * noise) if base else spread * noise
        out[name] = __import__('jax').numpy.asarray(drawn.astype(out[name].dtype))
    for name, factor in factors.items():
        out[name] = (out[name] * factor).astype(out[name].dtype)
    return out
```

```python
from contextlib import ExitStack

import concourse.bass as bass
import concourse.mybir as mybir
from concourse.alu_op_type import AluOpType as ALU

F32, F32R, BF16 = mybir.dt.float32, mybir.dt.float32r, mybir.dt.bfloat16
ACT = mybir.ActivationFunctionType

P = 128
D = 1024
TOK = 1024
NT = TOK // P
KT = D // P
FF = 4 * D
AW = 2 * D
GROUPS = 8
UC = 256
US = KT * UC
HALF = 512
HEADS, HD = 16, 64
EPS = 1e-6
SCALE = HD ** -0.5
MASKED = -1.0e30
PASSES = ((0, 0), (0, 1), (1, 0))

CH_A, CH_M = AW // UC, FF // UC
U_V = 0
U_A = U_V + AW // UC
U_M0 = U_A + 2 * CH_A
U_V2 = U_M0 + 2 * CH_M
U_QK = U_V2 + D // UC
U_O = U_QK + 2 * D // UC
U_M1 = U_O + D // UC
U_END = U_M1 + 2 * CH_M

FI_V = 0
FI_A = FI_V + NT * AW // UC
FI_M0 = FI_A + 4 * CH_A
FI_V2 = FI_M0 + 4 * CH_M
FI_QK = FI_V2 + NT * D // UC
FI_O = FI_QK + 4 * 2 * D // UC
FI_M1 = FI_O + NT * D // UC
ACT_GAP = FI_M1 - FI_V2
HB = 2 * NT

BI_SET = 0
BI_A = BI_SET + 4
BI_M0 = BI_A + 4 * CH_A + 16 * (CH_A - 1)
BI_M1 = BI_M0 + 16 * (CH_M - 1)

AI_A, AI_M0, AI_M1 = 0, 4 * CH_A, 4 * CH_A + 4 * CH_M


def wait(eng, sem, value):
    if isinstance(value, int) and value <= 0:
        return
    eng.wait_ge(sem, value)


def iterate(eng, n, emit):
    emit(0)
    if n > 2:
        with eng.Fori(1, n - 1) as i:
            emit(i)
    if n > 1:
        emit(n - 1)


def mix_item(c):
    return BI_A if isinstance(c, int) and c == 0 else c * 20 + (BI_A - 16)


def s_end(c, bi0, per, extra):
    return bi0 if isinstance(c, int) and c < 0 else c * per + (bi0 + extra + 16)


QP = NT // 2
GH = QP * (QP + 1) // 2


def groups_before(m):
    return (m // QP) * GH + (m % QP) * (m % QP + 1) // 2


def build(nc, x, g_mix_pre, g_mix_post, g_ffn_pre, g_ffn_post, w_in, v_g, v_b, w_s, b_s, w_aout,
          w_qkv, w_bout, w1, w2, out):
    ctx = ExitStack()
    with ctx:
        def sem(name):
            return ctx.enter_context(nc.semaphore(name))

        place = [-(-nc.sbuf_base // 64) * 64]

        def at(name, shape, dt, offset=None):
            size = 4 if dt != BF16 else 2
            for s in shape[1:]:
                size *= s
            if offset is None:
                offset = place[0]
                place[0] += -(-size // 32) * 32
                assert place[0] <= 229344, (name, place[0])
            return nc.alloc_sbuf_tensor_at(name, shape, dt, offset=offset)

        hT = [at("hT_hi", [P, KT, TOK], F32R), at("hT_lo", [P, KT, TOK], F32R)]
        o_acc = place[0]
        acc = at("acc", [P, NT, D], F32)
        o_a = place[0]
        a_buf = [[at(f"a{b}_{s}", [P, 2, TOK], F32R) for s in ("hi", "lo")] for b in range(2)]
        stage = at("stage", [P, US], F32)
        wt = [[at(f"w{b}_{s}", [P, US], F32R) for s in ("hi", "lo")] for b in range(2)]
        vring = at("vring", [P, 2, NT, UC], F32, o_acc)
        v2ring = [at(f"v2ring{b}", [P, 4, NT, 2, HD], F32R, o_acc + b * 16384) for b in range(2)]
        q_st = [at(f"q_st{b}", [P, TOK], F32R, o_acc + b * 16384) for b in range(2)]
        k_st = [[at(f"k_st{b}{s}", [P, TOK], F32R, o_acc + b * 16384 + 4096 * (s + 1)) for s in range(2)]
                for b in range(2)]
        v_st = [at(f"v_st{b}", [P, NT, 2 * HD], F32R, o_acc + b * 16384 + 12288) for b in range(2)]
        brk = [at(f"brk{b}", [P, TOK], F32, o_a + b * 4096) for b in range(4)]
        ws_nat = at("ws_nat", [P, GROUPS, P], F32, o_a)
        o_const = place[0]
        wsT = [at("wsT_hi", [P, GROUPS * P], F32R), at("wsT_lo", [P, GROUPS * P], F32R)]
        rs_bc = at("rs_bc", [P, GROUPS * P], F32)
        bs_bc = at("bs_bc", [P, GROUPS * P], F32)
        relu = [at(f"relu{b}", [P, HALF], F32, o_const + b * 2048) for b in range(2)]
        o_low = at("o_low", [HD, 2, HALF], F32, o_const)
        o_sum = at("o_sum", [P, 2, HALF], F32, o_const + 4096)
        stick = [at(f"stick{b}", [P, TOK + 8], F32, o_a + 16384 + b * 4128 if b < 3 else o_const + 8192)
                 for b in range(4)]
        o_scr = place[0]
        xt = [at(f"xt{b}", [P, D], F32) for b in range(4)]
        gpost = at("gpost", [P, D], F32)
        gpre = at("gpre", [P, D], F32)
        h_nat = [at(f"h_nat{b}", [P, D], F32) for b in range(2)]
        junk = at("junk", [P, D], BF16)
        vst = at("vst", [P, NT, UC], F32, o_scr)
        vn = [at("vn_hi", [P, NT, UC], F32R, o_scr + 8192), at("vn_lo", [P, NT, UC], F32R, o_scr + 16384)]
        ut = at("ut", [P, 4, HALF], F32, o_scr + 24576)
        bb = at("bb", [P, 2, P], F32, o_scr + 32768)
        aT = [[at(f"aT{q}_{s}", [P, (3 + q) * HALF], F32R, o_scr + q * 12288 + n * (3 + q) * 2048)
               for n, s in enumerate(("hi", "lo"))] for q in range(2)]
        ident = at("ident", [P, P], F32)
        ident_bf = at("ident_bf", [P, P], BF16)
        mask_bf = at("mask_bf", [P, P], BF16)
        ones = at("ones", [P, P], F32R)
        eps = at("eps", [P, 1], F32)
        stats = at("stats", [P, NT, AW // UC, 6], F32)
        mv = at("mv", [P, NT, 2], F32)
        v_rt = at("v_rt", [P, NT], F32)
        v_rs = at("v_rs", [P, NT], F32)
        vg_c = at("vg_c", [P, AW // P], F32)
        vb_c = at("vb_c", [P, AW // P], F32)
        ss = at("ss", [P, 2, NT], F32)
        rt = at("rt", [P, 2, NT], F32)
        rstd = at("rstd", [P, 2, NT], F32)

        psum = ctx.enter_context(nc.psum_tensor("psum", [P, 8, HALF], F32))
        z_ps = [psum[:, 2 * b:2 * b + 2, :].rearrange("p a n -> p (a n)") for b in range(2)]

        xres = [nc.dram_tensor(f"x_res{n}", (TOK, D), F32, kind="Internal").ap() for n in range(3)]
        v_dram = nc.dram_tensor("v_gelu", (AW // UC, P, NT * UC), F32, kind="Internal").ap()
        qk_dram = [nc.dram_tensor(f"qk_{s}", (2 * D, TOK), F32R, kind="Internal").ap() for s in ("hi", "lo")]
        v2_dram = nc.dram_tensor("v_heads", (HEADS, P, NT * 2 * HD), F32R, kind="Internal").ap()

        def rows(ap):
            return ap.rearrange("(t p) n -> t p n", p=P)

        x_from = [rows(x), rows(x), rows(xres[0]), rows(xres[1]), rows(xres[2])]
        x_to = [None, rows(xres[0]), rows(xres[1]), rows(xres[2]), rows(out)]

        unit_landed = sem("unit_landed")
        unit_hi = sem("unit_hi")
        unit_ready = sem("unit_ready")
        front_psum = sem("front_psum")
        act_evac = sem("act_evac")
        dve_evac = sem("dve_evac")
        front_hi = sem("front_hi")
        hT_psum = sem("hT_psum")
        hT_done = sem("hT_done")
        back_psum = sem("back_psum")
        back_evac = sem("back_evac")
        ch_hi = sem("ch_hi")
        ch_lo = sem("ch_lo")
        relu_sq = sem("relu_sq")
        consts = sem("consts")
        eps_set = sem("eps_set")
        vecs = sem("vecs")
        ws_in = sem("ws_in")
        ws_masked = sem("ws_masked")
        ws_hi = sem("ws_hi")
        x_in = [sem(f"x_in{b}") for b in range(4)]
        g_in = sem("g_in")
        x_out = sem("x_out")
        m_sq = sem("m_sq")
        m_rt = sem("m_rt")
        post = sem("post")
        x_sq = sem("x_sq")
        x_rt = sem("x_rt")
        pre = sem("pre")
        v_stats = sem("v_stats")
        v_out = [sem(f"v_out{b}") for b in range(2)]
        v_norm = sem("v_norm")
        v_sqrt = sem("v_sqrt")
        v_in = sem("v_in")
        vn_nat = sem("vn_nat")
        vn_hi = sem("vn_hi")
        vn_lo = sem("vn_lo")
        bb_set = sem("bb_set")
        gate = sem("gate")
        qk_out = [sem(f"qk_out{b}") for b in range(2)]
        v2_out = [sem(f"v2_out{b}") for b in range(2)]
        qk_in = [sem(f"qk_in{b}") for b in range(2)]
        vh_in = [sem(f"vh_in{b}") for b in range(2)]
        z_done = sem("z_done")
        keep_done = sem("keep_done")
        brk_done = sem("brk_done")
        rows_set = sem("rows_set")
        stick_done = sem("stick_done")
        a_done = sem("a_done")
        aT_psum = sem("aT_psum")
        aT_hi = sem("aT_hi")
        aT_lo = sem("aT_lo")
        av_done = sem("av_done")
        o_lo = sem("o_lo")
        o_add = sem("o_add")
        o_hi = sem("o_hi")
        o_split = sem("o_split")

        block = ctx.enter_context(nc.Block())

        def cols(w, c):
            return w.rearrange("(k p) f -> p k f", p=P)[:, :, bass.ds(c * UC, UC)]

        def rws(w, c):
            return w.rearrange("(r p) n -> p r n", p=P)[:, bass.ds(c * 2, 2), :]

        stage_c = stage[:].rearrange("p (k f) -> p k f", k=KT)
        stage_r = stage[:].rearrange("p (r n) -> p r n", r=2)

        @block.sync
        def _(sp):
            def unit(n, src, dst):
                wait(sp, unit_ready, n)
                sp.dma_start(dst, src).then_inc(unit_landed, 16)

            def load_x(b, t):
                if t >= 4:
                    if b < 4:
                        sp.wait_ge(pre, 2 * (NT * b + t - 3))
                    if b:
                        sp.wait_ge(x_out, 16 * (NT * (b - 1) + t - 3))
                elif t == 0:
                    wait(sp, pre, 2 * NT * b)
                    wait(sp, x_out, 16 * NT * (b - 1))
                sp.dma_start(xt[t % 4][:], x_from[b][t]).then_inc(x_in[t % 4], 16)

            def load_g(b):
                wait(sp, pre, 2 * NT * min(b, 4))
                if b:
                    g = (g_mix_post, g_ffn_post)[(b - 1) % 2][(b - 1) // 2:(b - 1) // 2 + 1, :]
                    sp.dma_start(gpost[:], g.to_broadcast([P, D])).then_inc(g_in, 16)
                if b < 4:
                    g = (g_mix_pre, g_ffn_pre)[b % 2][b // 2:b // 2 + 1, :]
                    sp.dma_start(gpre[:], g.to_broadcast([P, D])).then_inc(g_in, 16)

            def boundary(b):
                for t in range(NT):
                    if b:
                        wait(sp, post, 3 * (NT * (b - 1) + t + 1))
                        sp.dma_start(x_to[b][t], xt[t % 4][:]).then_inc(x_out, 16)
                    if t + 4 < NT:
                        load_x(b, t + 4)

            def chunks(u0, c_n, up, up_col, down, scratch_v=False):
                def load_up(c):
                    unit(u0 + 2 * c - (0 if isinstance(c, int) and c == 0 else 1), cols(up, c + up_col), stage_c)
                    if scratch_v:
                        wait(sp, vn_lo, c)
                        if isinstance(c, int) and c == 0:
                            for b in range(2):
                                wait(sp, v_out[b], 16 * AW // UC // 2)
                            wait(sp, pre, 2 * NT)
                            wait(sp, hT_psum, HB)
                        sp.dma_start(vst[:].rearrange("p t f -> p (t f)"),
                                     v_dram[bass.ds(c, 1)].rearrange("o p f -> (o p) f")).then_inc(v_in, 16)

                def step(i):
                    if isinstance(i, int) and i == 0:
                        load_up(0)
                    load_up(2 * i + 1)
                    unit(u0 + 2 + 4 * i, rws(down, 2 * i), stage_r)
                    if not (isinstance(i, int) and i == c_n // 2 - 1):
                        load_up(2 * i + 2)
                        unit(u0 + 4 + 4 * i, rws(down, 2 * i + 1), stage_r)
                iterate(sp, c_n // 2, step)
                unit(u0 + 2 * c_n - 1, rws(down, c_n - 1), stage_r)

            load_x(0, 0)
            load_g(0)
            load_x(0, 1)
            unit(U_V, cols(w_in, AW // UC), stage_c)
            for t in range(2, 4):
                load_x(0, t)
            boundary(0)
            unit(U_V + 1, cols(w_in, AW // UC + 1), stage_c)
            sp.dma_start(ws_nat[:], w_s.rearrange("g t s -> t g s")).then_inc(ws_in, 16)
            sp.dma_start(bs_bc[:], b_s.rearrange("(o g) t -> o (g t)", o=1).to_broadcast([P, GROUPS * P])).then_inc(vecs, 16)
            with nc.allow_non_contiguous_dma("two vectors of 2048 values"):
                sp.dma_start(vg_c[:], v_g.rearrange("o (c p) -> p (o c)", p=P)).then_inc(vecs, 16)
                sp.dma_start(vb_c[:], v_b.rearrange("o (c p) -> p (o c)", p=P)).then_inc(vecs, 16)

            with sp.Fori(2, AW // UC) as u:
                unit(U_V + u, cols(w_in, u + AW // UC), stage_c)
            chunks(U_A, CH_A, w_in, 0, w_aout, scratch_v=True)
            wait(sp, ch_lo, AI_A + 4 * CH_A)
            for t in range(4):
                load_x(1, t)
            load_g(1)
            unit(U_M0, cols(w1[0], 0), stage_c)
            boundary(1)
            def mlp_rest(u0, layer):
                def load_up(c):
                    unit(u0 + 2 * c - 1, cols(w1[layer], c), stage_c)

                def step(i):
                    load_up(2 * i + 1)
                    unit(u0 + 2 + 4 * i, rws(w2[layer], 2 * i), stage_r)
                    if not (isinstance(i, int) and i == CH_M // 2 - 1):
                        load_up(2 * i + 2)
                        unit(u0 + 4 + 4 * i, rws(w2[layer], 2 * i + 1), stage_r)
                iterate(sp, CH_M // 2, step)

            mlp_rest(U_M0, 0)
            load_g(2)
            for t in range(4):
                load_x(2, t)
            unit(U_V2 - 1, rws(w2[0], CH_M - 1), stage_r)
            unit(U_V2, cols(w_qkv, 2 * D // UC), stage_c)
            boundary(2)
            with sp.Fori(1, D // UC) as u:
                unit(U_V2 + u, cols(w_qkv, u + 2 * D // UC), stage_c)
            with sp.Fori(0, 2 * D // UC) as u:
                unit(U_QK + u, cols(w_qkv, u), stage_c)
            unit(U_O, cols(w_bout, 0), stage_c)

            def load_qk(h, b):
                wait(sp, z_done, h * NT - NT)
                for s in range(2):
                    r = slice(s * HD, (s + 1) * HD)
                    sp.dma_start(q_st[b][r, :].bitcast(F32), qk_dram[s][bass.ds(h * HD, HD), :].bitcast(F32)).then_inc(qk_in[b], 16)
                    for s2 in range(2):
                        sp.dma_start(k_st[b][s2][r, :].bitcast(F32), qk_dram[s2][bass.ds(h * HD + D, HD), :].bitcast(F32)).then_inc(qk_in[b], 16)

            def load_v(h, b):
                wait(sp, av_done, h * GH - GH)
                sp.dma_start(v_st[b][:].rearrange("p t d -> p (t d)").bitcast(F32),
                             v2_dram[bass.ds(h, 1)].rearrange("o p f -> (o p) f").bitcast(F32)).then_inc(vh_in[b], 16)

            for b in range(2):
                wait(sp, v2_out[b], 64 * (D // UC) // 2)
            wait(sp, qk_out[0], 32 * ((D // UC) // 2 + 1))
            for h in range(2):
                load_qk(h, h)
                load_v(h, h)
            unit(U_O + 1, cols(w_bout, 1), stage_c)
            for b in range(2):
                wait(sp, qk_out[b], 32 * (2 * D // UC) // 2)
            unit(U_O + 2, cols(w_bout, 2), stage_c)
            with sp.Fori(1, HEADS // 2) as i:
                for b in range(2):
                    load_qk(2 * i + b, b)
                    load_v(2 * i + b, b)
            wait(sp, o_split, 2 * HEADS)
            load_g(3)
            for t in range(4):
                load_x(3, t)
            unit(U_O + 3, cols(w_bout, 3), stage_c)
            unit(U_M1, cols(w1[1], 0), stage_c)
            boundary(3)
            mlp_rest(U_M1, 1)
            load_g(4)
            for t in range(4):
                load_x(4, t)
            unit(U_END - 1, rws(w2[1], CH_M - 1), stage_r)
            boundary(4)
            wait(sp, x_out, 16 * NT * 4)

        @block.gpsimd
        def _(pool):
            pool.memset(eps[:], EPS).then_inc(eps_set, 1)
            pool.memset(ident[:], 0.0).then_inc(consts, 1)
            pool.memset(mask_bf[:], 0.0).then_inc(consts, 1)
            pool.memset(ones[:].bitcast(F32), 1.0).then_inc(consts, 1)
            pool.wait_ge(consts, 2)
            pool.affine_select(out=ident[:], in_=ident[:], compare_op=ALU.not_equal, fill=1.0, base=0,
                               pattern=[[-1, P]], channel_multiplier=1).then_inc(consts, 1)
            pool.affine_select(out=mask_bf[:], in_=mask_bf[:], compare_op=ALU.is_gt, fill=MASKED, base=0,
                               pattern=[[-1, P]], channel_multiplier=1).then_inc(consts, 1)
            pool.wait_ge(eps_set, 1)
            pool.wait_ge(consts, 4)
            pool.tensor_copy(ident_bf[:], ident[:]).then_inc(consts, 1)

            def lo(n, b):
                pool.wait_ge(unit_hi, n + 1)
                pool.tensor_tensor(wt[b][1][:], stage[:], wt[b][0][:].bitcast(F32), ALU.subtract).then_inc(unit_ready, 1)

            lo(0, 0)
            pool.wait_ge(ws_in, 16)
            pool.affine_select(out=ws_nat[:], in_=ws_nat[:], compare_op=ALU.is_ge, fill=0.0, base=0,
                               pattern=[[0, GROUPS], [-1, P]], channel_multiplier=1).then_inc(ws_masked, 1)
            lo(1, 1)
            with pool.Fori(1, (U_O + 2) // 2) as i:
                lo(2 * i, 0)
                lo(2 * i + 1, 1)

            def stick_mult(k, r):
                s = (k % NT + 1) * P
                pool.wait_ge(brk_done, r + k + 1)
                pool.wait_ge(stick_done, r + k + 1)
                pool.tensor_tensor(brk[k % 4][:, TOK - s:TOK], brk[k % 4][:, TOK - s:TOK],
                                   stick[k % 4][:, TOK + 1 - s:TOK + 1], ALU.mult).then_inc(a_done, 1)

            with pool.Fori(0, HEADS // 2) as i:
                for k in range(2 * NT):
                    stick_mult(k, i * (2 * NT))
            with pool.Fori((U_O + 2) // 2, U_END // 2) as i:
                lo(2 * i, 0)
                lo(2 * i + 1, 1)

        @block.tensor
        def _(pe):
            def t_item(evac, fi, bank, ub, f, half):
                wait(pe, evac[0], fi - (3 + evac[1]))
                n = 0
                for k in range(KT):
                    for sw, sh in PASSES:
                        mm = pe.matmul(psum[:, bank, :], wt[ub][sw][:, k * UC + f * P:k * UC + (f + 1) * P],
                                       hT[sh][:, k, half * HALF:(half + 1) * HALF],
                                       start=(n == 0), stop=(n == 3 * KT - 1))
                        n += 1
                return mm

            def n_item(evac, fi, bank, ub, t, before=3, c0=0):
                if before is not None:
                    wait(pe, evac[0], fi - (before + evac[1]))
                n = 0
                for k in range(KT):
                    for sh, sw in PASSES:
                        mm = pe.matmul(psum[:, bank, c0:c0 + UC], hT[sh][:, k, t * P:(t + 1) * P],
                                       wt[ub][sw][:, k * UC:(k + 1) * UC],
                                       start=(n == 0), stop=(n == 3 * KT - 1))
                        n += 1
                return mm

            def s_item(bi, bank, parts, t, n2):
                wait(pe, back_evac, bi - 3)
                todo = [(ab, ub, r, sa, sw) for ab, ub in parts for r in range(2) for sa, sw in PASSES]
                for n, (ab, ub, r, sa, sw) in enumerate(todo):
                    mm = pe.matmul(psum[:, 4 + bank, :], a_buf[ab][sa][:, r, t * P:(t + 1) * P],
                                   wt[ub][sw][:, r * D + n2 * HALF:r * D + (n2 + 1) * HALF],
                                   start=(n == 0), stop=(n == len(todo) - 1))
                return mm

            def transposes(b, t):
                pe.wait_ge(pre, 2 * (NT * b + t + 1))
                for q in range(2):
                    wait(pe, hT_done, HB * b + 2 * t + q - 1)
                    for j in range(4):
                        k = 4 * q + j
                        mm = pe.transpose(psum[:, 2 + q, j * P:(j + 1) * P], h_nat[t % 2][:, k * P:(k + 1) * P], ident[:])
                    mm.then_inc(hT_psum, 1)

            def ready(n):
                pe.wait_ge(unit_ready, n + 1)

            ACT_EV, DVE_EV = (act_evac, 0), (dve_evac, FI_V2)

            pe.wait_ge(consts, 6)
            for t in range(NT // 2):
                transposes(0, t)
            ready(U_V)
            for t in range(NT):
                pe.wait_ge(hT_done, 2 * t + 2)
                n_item(ACT_EV, FI_V + t, 4 + t // 2, 0, t, None, (t % 2) * UC).then_inc(front_psum, 1)
                if t + NT // 2 < NT:
                    transposes(0, t + NT // 2)

            ready(U_V + 1)
            for t in range(NT):
                n_item(ACT_EV, FI_V + NT + t, t % 4, 1, t, None if t < 4 else 3).then_inc(front_psum, 1)
                if t == 3:
                    pe.wait_ge(ws_masked, 1)
                    pe.wait_ge(act_evac, FI_V + NT)
                    for q in range(2):
                        for j in range(4):
                            mm = pe.transpose(psum[:, 4 + q, j * P:(j + 1) * P], ws_nat[:, 4 * q + j, :], ident[:])
                        mm.then_inc(back_psum, 1)
            for q in range(2):
                pe.wait_ge(back_evac, q + 1)
                for s in range(2):
                    mm = pe.matmul(psum[:, 6 + q, :], ones[:], wsT[s][:, q * HALF:(q + 1) * HALF],
                                   start=(s == 0), stop=(s == 1))
                mm.then_inc(back_psum, 1)

            def n_units(evac, u0, fi0, i):
                for b in range(2):
                    ready(i * 2 + (u0 + b))
                    for t in range(NT):
                        n_item(evac, i * (2 * NT) + (fi0 + NT * b + t), t % 4, b, t).then_inc(front_psum, 1)

            with pe.Fori(1, AW // UC // 2) as i:
                n_units(ACT_EV, U_V, FI_V, i)

            def chunk_phase(u0, fi0, bi0, ai0, c_n, mix, tail, norm=None, gap=0):
                per = 20 if mix else 16

                def up(c, first=False):
                    if first and norm is not None:
                        transposes(norm, NT - 2)
                    ready(u0 + 2 * c - (0 if first else 1))
                    if first and norm is not None:
                        pe.wait_ge(hT_done, HB * norm + NT)
                    for half in range(2):
                        if first and norm is not None and half:
                            pe.wait_ge(hT_done, HB * (norm + 1))
                        for f in range(2):
                            j = 2 * half + f
                            t_item((act_evac, gap), c * 4 + (fi0 + j), j, 0 if first else 1, f, half).then_inc(front_psum, 1)
                            if first and norm is not None and j == 0:
                                transposes(norm, NT - 1)
                    if mix:
                        pe.wait_ge(vn_lo, c + 1)
                        for half in range(2):
                            for f in range(2):
                                j = 2 * half + f
                                bi = mix_item(c) + j
                                wait(pe, back_evac, bi - 3)
                                for t in range(4 * half, 4 * half + 4):
                                    for n, (sv, sw) in enumerate(PASSES):
                                        mm = pe.matmul(psum[:, 4 + j, (t % 4) * P:(t % 4 + 1) * P],
                                                       vn[sv][:, t, f * P:(f + 1) * P],
                                                       wsT[sw][:, bass.ds(c * P, P)], start=(n == 0), stop=(n == 2))
                                mm.then_inc(back_psum, 1)

                def down(c, ab):
                    ready(u0 + 2 * c + 2)
                    pe.wait_ge(ch_lo, c * 4 + (ai0 + 4))
                    for j in range(16):
                        bi = c * per + (bi0 + j + (8 if mix else 0))
                        mm = s_item(bi, j % 4, [(ab, 0)], j // 2, j % 2)
                        mm.then_inc(back_psum, 1)

                def step(i):
                    if isinstance(i, int) and i == 0:
                        up(0, first=True)
                    up(2 * i + 1)
                    if isinstance(i, int) and i == c_n // 2 - 1:
                        return
                    down(2 * i, 0)
                    up(2 * i + 2)
                    down(2 * i + 1, 1)
                iterate(pe, c_n // 2, step)

                c = c_n - 2
                ready(u0 + 2 * c + 2)
                ready(u0 + 2 * c + 3)
                pe.wait_ge(ch_lo, ai0 + 4 * c_n)
                for t in range(NT):
                    for n2 in range(2):
                        bi = c * per + (bi0 + 2 * t + n2 + (8 if mix else 0))
                        mm = s_item(bi, (2 * t + n2) % 4, [(0, 0), (1, 1)], t, n2)
                        mm.then_inc(back_psum, 1)
                    if tail is not None and t >= 2:
                        transposes(tail, t - 2)

            chunk_phase(U_A, FI_A, BI_A, AI_A, CH_A, True, 1)
            chunk_phase(U_M0, FI_M0, BI_M0, AI_M0, CH_M, False, 2, norm=1)
            transposes(2, NT - 2)

            pe.wait_ge(act_evac, FI_V2)
            ready(U_V2)
            for t in range(NT):
                pe.wait_ge(hT_done, 2 * HB + 2 * t + 2)
                n_item(DVE_EV, FI_V2 + t, t % 2, 0, t, 1).then_inc(front_psum, 1)
                if t == 1:
                    transposes(2, NT - 1)
            ready(U_V2 + 1)
            for t in range(NT):
                before = 3 if t >= 4 else 1 if t < 2 else None
                n_item(DVE_EV, FI_V2 + NT + t, t % 4, 1, t, before).then_inc(front_psum, 1)
            with pe.Fori(1, D // UC // 2) as i:
                n_units(DVE_EV, U_V2, FI_V2, i)

            with pe.Fori(0, D // UC) as i:
                for b in range(2):
                    ready(i * 2 + (U_QK + b))
                    for j in range(4):
                        t_item(DVE_EV, i * 8 + (FI_QK + 4 * b + j), j, b, j % 2, j // 2).then_inc(front_psum, 1)

            pe.wait_ge(dve_evac, FI_O - FI_V2)
            pe.wait_ge(back_evac, BI_M1)

            def scores(i, k):
                hb, tb, zb = (k // NT) % 2, k % NT, k % 2
                if tb == 0:
                    pe.wait_ge(qk_in[hb], (i + k // (2 * NT)) * (6 * 16) + 6 * 16)
                wait(pe, brk_done, i * (2 * NT) + (k - 1))
                s = (tb + 1) * P
                for c0 in range(0, s, HALF):
                    c1 = c0 + max(2 * P, min(HALF, s - c0))
                    for n in range(2):
                        mm = pe.matmul(z_ps[zb][:, c0:c1], q_st[hb][:, tb * P:(tb + 1) * P], k_st[hb][n][:, c0:c1],
                                       start=(n == 0), stop=(n == 1 and c1 < s))
                mm = pe.matmul(z_ps[zb][:, s - P:s], ident_bf[:], mask_bf[:], start=False, stop=True)
                mm.then_inc(z_done, 1)

            def to_keys(i, m, g):
                mh, gi = m % QP, groups_before(m) + g
                if g == 0:
                    pe.wait_ge(a_done, i * (2 * NT) + (2 * m + 2))
                wait(pe, aT_lo, i * (2 * GH) + (gi - 1))
                for p in (2 * g, 2 * g + 1):
                    for e in range(2):
                        if p == 0 and e == 0:
                            continue
                        col = TOK - (2 * mh + e + 1) * P + (2 * mh + 1 - p) * P
                        at_col = (p % 2) * 2 * P + e * P
                        mm = pe.transpose(psum[:, 4 + gi % 2, at_col:at_col + P],
                                          brk[(2 * m + e) % 4][:, col:col + P], ident[:])
                mm.then_inc(aT_psum, 1)

            def values(i, m, g):
                mh, hb = m % QP, (m // QP) % 2
                if g == 0 and mh == 0:
                    pe.wait_ge(vh_in[hb], i * 16 + 16)
                if g == 0 and mh % 2 == 0:
                    wait(pe, o_add, i * 4 + (m // 2 - 1))
                pe.wait_ge(aT_lo, i * (2 * GH) + (groups_before(m) + g + 1))
                for p in (2 * g, 2 * g + 1):
                    for s in range(2):
                        mm = pe.matmul(psum[:, 6 + mh // 2, (mh % 2) * 2 * P:(mh % 2 + 1) * 2 * P],
                                       v_st[hb][:, 2 * mh + 1 - p, :], aT[m % 2][s][:, p * 2 * P:(p + 1) * 2 * P],
                                       start=(p == 0 and s == 0), stop=(p == 2 * mh + 1 and s == 1))
                mm.then_inc(av_done, 1)

            def att_step(i):
                first, last = isinstance(i, int) and i == 0, isinstance(i, int) and i == HEADS // 2 - 1
                if first:
                    scores(0, 0)
                    scores(0, 1)
                    pe.wait_ge(rows_set, 8)
                for m in range(2 * QP):
                    if not (last and m == 2 * QP - 1):
                        scores(i, 2 * m + 2)
                        scores(i, 2 * m + 3)
                    before = 0 if first and m == 0 else (m - 1) % QP + 1
                    for g in range(max(m % QP + 1, before)):
                        if g < m % QP + 1:
                            to_keys(i, m, g)
                        if g < before:
                            if m:
                                values(i, m - 1, g)
                            else:
                                values(i - 1, 2 * QP - 1, g)
            iterate(pe, HEADS // 2, att_step)
            for g in range(QP):
                values(HEADS // 2 - 1, 2 * QP - 1, g)

            pe.wait_ge(o_split, 2 * HEADS)
            pe.wait_ge(brk_done, HEADS * NT)
            for u in range(D // UC):
                ready(U_O + u)
                last = u == D // UC - 1
                for t in range(NT):
                    before = 3 if not last or t < 2 else 1
                    n_item(DVE_EV, FI_O + u * NT + t, t % (2 if last else 4), u % 2, t, before).then_inc(front_psum, 1)
                    if last and t >= 2:
                        if t == 2:
                            pe.wait_ge(dve_evac, FI_M1 - NT - FI_V2)
                        transposes(3, t - 2)
            pe.wait_ge(dve_evac, FI_M1 - FI_V2)
            chunk_phase(U_M1, FI_M1, BI_M1, AI_M1, CH_M, False, None, norm=3, gap=ACT_GAP)

        @block.scalar
        def _(act):
            def hi(n, b):
                act.wait_ge(unit_landed, n * 16 + 16)
                act.activation(wt[b][0][:], stage[:], ACT.Copy).then_inc(unit_hi, 1)

            def square_m(b, t):
                n = NT * (b - 1) + t
                if b == 3:
                    act.wait_ge(dve_evac, FI_M1 - FI_V2 - NT + t + 1)
                else:
                    act.wait_ge(back_evac, TAIL[b] + 2 * t + 2)
                wait(act, m_sq, n)
                act.wait_ge(x_sq, NT * b + t if b < 4 else NT * 4)
                act.activation(junk[:], acc[:, t, :], ACT.Square, accum_out=ss[:, 0, t:t + 1]).then_inc(m_sq, 1)
                act.wait_ge(m_sq, n + 1)
                act.activation(rt[:, 0, t:t + 1], ss[:, 0, t:t + 1], ACT.Sqrt, bias=eps[:, 0:1], scale=1.0 / D).then_inc(m_rt, 1)

            def square_x(b, t):
                n = NT * b + t
                if b:
                    act.wait_ge(post, 3 * (n - NT + 1))
                else:
                    act.wait_ge(x_in[t % 4], 16 * (t // 4 + 1))
                wait(act, x_sq, n)
                if b:
                    act.wait_ge(m_sq, n - NT + 1)
                act.activation(junk[:], xt[t % 4][:], ACT.Square, accum_out=ss[:, 1, t:t + 1]).then_inc(x_sq, 1)
                act.wait_ge(x_sq, n + 1)
                act.activation(rt[:, 1, t:t + 1], ss[:, 1, t:t + 1], ACT.Sqrt, bias=eps[:, 0:1], scale=1.0 / D).then_inc(x_rt, 1)

            def take_hi(b, t):
                for q in range(2):
                    act.wait_ge(hT_psum, HB * b + 2 * t + q + 1)
                    act.activation(hT[0][:, 4 * q:4 * q + 4, t * P:(t + 1) * P],
                                   psum[:, 2 + q, :].rearrange("p (k n) -> p k n", k=4), ACT.Copy).then_inc(front_hi, 1)

            def boundary(b, u_next=None, freed=None):
                for t in range(NT):
                    if b == 3 and t == 0:
                        act.wait_ge(front_psum, FI_O + 3 * NT)
                        hi(u_next, 0)
                    if b in (1, 2) and t == NT - 1:
                        act.wait_ge(*freed)
                        hi(u_next, 0)
                    square_m(b, t)
                    if b < 4:
                        if t >= 2:
                            take_hi(b, t - 2)
                        square_x(b, t)
                if b < 4:
                    take_hi(b, NT - 2)
                    take_hi(b, NT - 1)
                    act.wait_ge(*freed)
                    hi(u_next + 1, 1)

            act.wait_ge(eps_set, 1)
            for t in range(NT + 1):
                if t < NT:
                    square_x(0, t)
                if t:
                    take_hi(0, t - 1)
                if t == 2:
                    hi(U_V, 0)
            hi(U_V + 1, 1)

            def v_store(u, b):
                act.dma_start(v_dram[bass.ds(u, 1)].rearrange("o p f -> (o p) f"),
                              vring[:, b].rearrange("p t f -> p (t f)")).then_inc(v_out[b], 16)

            for t in range(NT):
                act.wait_ge(front_psum, FI_V + t + (2 if t % 2 == 0 else 1))
                act.activation(vring[:, 0, t, :], psum[:, 4 + t // 2, (t % 2) * UC:(t % 2 + 1) * UC],
                               ACT.Gelu).then_inc(act_evac, 1)
            hi(U_V + 2, 0)
            act.wait_ge(act_evac, FI_V + NT)
            v_store(0, 0)
            for t in range(NT):
                act.wait_ge(front_psum, FI_V + NT + t + 1)
                act.activation(vring[:, 1, t, :], psum[:, t % 4, 0:UC], ACT.Gelu).then_inc(act_evac, 1)
                if t == 3:
                    for q in range(2):
                        act.wait_ge(back_psum, q + 1)
                        act.activation(wsT[0][:, q * HALF:(q + 1) * HALF], psum[:, 4 + q, :], ACT.Copy).then_inc(ws_hi, 1)
            hi(U_V + 3, 1)
            act.wait_ge(act_evac, FI_V + 2 * NT)
            v_store(1, 1)

            def v_units(i, last=False):
                for b in range(2):
                    act.wait_ge(v_out[b], i * 16)
                    act.wait_ge(v_stats, i * (2 * NT) + (b - 1) * NT)
                    for t in range(NT):
                        act.wait_ge(front_psum, i * (2 * NT) + (FI_V + b * NT + t + 1))
                        act.activation(vring[:, b, t, :], psum[:, t % 4, 0:UC], ACT.Gelu).then_inc(act_evac, 1)
                    if not (last and b):
                        hi(i * 2 + (U_V + b + 2), b)
                    act.wait_ge(act_evac, i * (2 * NT) + (FI_V + (b + 1) * NT))
                    v_store(2 * i + b, b)

            with act.Fori(1, AW // UC // 2 - 1) as i:
                v_units(i)
            v_units(AW // UC // 2 - 1, last=True)
            act.wait_ge(v_norm, NT)
            act.activation(v_rt[:], mv[:, :, 1], ACT.Sqrt, bias=eps[:, 0:1], scale=1.0).then_inc(v_sqrt, 1)

            def gate_chunk(c, ab):
                if not (isinstance(c, int) and c == 0):
                    act.wait_ge(back_psum, s_end(c - 2, BI_A, 20, 8))
                    hi(c * 2 + U_A, 0)
                wait(act, vn_nat, c + 1)
                if not (isinstance(c, int) and c == 0):
                    act.wait_ge(back_psum, mix_item(c - 1) + 4)
                act.activation(vn[0][:], vst[:], ACT.Copy).then_inc(vn_hi, 1)
                for j in range(4):
                    act.wait_ge(front_psum, c * 4 + (FI_A + j + 1))
                    wait(act, ch_lo, c * 4 + (j - 3))
                    act.activation(ut[:, j, :], psum[:, j, :], ACT.Gelu).then_inc(act_evac, 1)
                hi(c * 2 + (U_A + 1), 1)
                for j in range(4):
                    act.wait_ge(back_evac, mix_item(c) + (j + 1))
                    act.wait_ge(back_psum, s_end(c - 2, BI_A, 20, 8))
                    act.activation(a_buf[ab][0][:, j % 2, (j // 2) * HALF:(j // 2 + 1) * HALF], ut[:, j, :],
                                   ACT.Copy).then_inc(ch_hi, 1)

            def gate_step(i):
                if isinstance(i, int) and i == 0:
                    gate_chunk(0, 0)
                gate_chunk(2 * i + 1, 1)
                if not (isinstance(i, int) and i == CH_A // 2 - 1):
                    gate_chunk(2 * i + 2, 0)
            iterate(act, CH_A // 2, gate_step)
            boundary(1, U_M0, (back_psum, BI_M0))

            def mlp(u0, fi0, ai0, bi0, gap=0):
                def chunk(c, ab):
                    if not (isinstance(c, int) and c == 0):
                        act.wait_ge(back_psum, s_end(c - 2, bi0, 16, 0))
                        hi(c * 2 + u0, 0)
                    for j in range(4):
                        act.wait_ge(front_psum, c * 4 + (fi0 + j + 1))
                        wait(act, ch_lo, c * 4 + (ai0 + j - 1))
                        act.activation(relu[j % 2][:], psum[:, j, :], ACT.Relu).then_inc(act_evac, 1)
                        act.wait_ge(act_evac, c * 4 + (fi0 - gap + j + 1))
                        act.wait_ge(back_psum, s_end(c - 2, bi0, 16, 0))
                        act.activation(a_buf[ab][0][:, j % 2, (j // 2) * HALF:(j // 2 + 1) * HALF], relu[j % 2][:],
                                       ACT.Square).then_inc(ch_hi, 1)
                    if not (isinstance(c, int) and c == 0):
                        hi(c * 2 + (u0 + 1), 1)

                def step(i):
                    if isinstance(i, int) and i == 0:
                        chunk(0, 0)
                    chunk(2 * i + 1, 1)
                    if not (isinstance(i, int) and i == CH_M // 2 - 1):
                        chunk(2 * i + 2, 0)
                iterate(act, CH_M // 2, step)

            mlp(U_M0, FI_M0, AI_M0, BI_M0)
            boundary(2, U_V2, (back_psum, BI_M1))

            for u in range(D // UC):
                b = u % 2
                if u >= 2:
                    act.wait_ge(v2_out[b], 64 * (u // 2))
                for t in range(NT):
                    act.wait_ge(front_psum, FI_V2 + u * NT + t + 1)
                    act.activation(v2ring[b][:, :, t, 0, :],
                                   psum[:, t % (4 if u else 2), 0:UC].rearrange("p (h d) -> p h d", h=4),
                                   ACT.Copy).then_inc(front_hi, 1)
                hi(U_V2 + u + 2, b)
                act.wait_ge(dve_evac, (u + 1) * NT)
                for j in range(4):
                    act.dma_start(v2_dram[4 * u + j].bitcast(F32),
                                  v2ring[b][:, j].rearrange("p t s d -> p (t s d)").bitcast(F32)).then_inc(v2_out[b], 16)

            def qk_step(i):
                for b in range(2):
                    if not (isinstance(i, int) and i == 0):
                        act.wait_ge(qk_out[b], i * 32)
                    for j in range(4):
                        act.wait_ge(front_psum, i * 8 + (FI_QK + 4 * b + j + 1))
                        act.activation(a_buf[b][0][:, j % 2, (j // 2) * HALF:(j // 2 + 1) * HALF], psum[:, j, :],
                                       ACT.Copy).then_inc(front_hi, 1)
                    hi(i * 2 + (U_QK + b + 2), b)
                    act.wait_ge(dve_evac, i * 8 + (FI_QK - FI_V2 + 4 * b + 4))
                    for s in range(2):
                        act.dma_start(qk_dram[s].rearrange("(u p) n -> p u n", p=P)[:, bass.ds(4 * i + 2 * b, 2), :].bitcast(F32),
                                      a_buf[b][s][:].bitcast(F32)).then_inc(qk_out[b], 16)
            qk_step(0)
            with act.Fori(1, D // UC) as i:
                qk_step(i)
            for b in range(2):
                act.wait_ge(qk_out[b], 32 * (2 * D // UC) // 2)
            act.wait_ge(x_out, 16 * NT * 2)

            def keep_tile(i, k):
                s = (k % NT + 1) * P
                act.wait_ge(z_done, i * (2 * NT) + (k + 1))
                wait(act, a_done, i * (2 * NT) + (k - 3))
                act.activation(stick[k % 4][:, TOK - s:TOK], z_ps[k % 2][:, 0:s], ACT.Sigmoid, scale=-SCALE).then_inc(keep_done, 1)

            def break_tile(i, k):
                s = (k % NT + 1) * P
                wait(act, aT_psum, i * (2 * GH) + groups_before(k // 2 - 1))
                act.activation(brk[k % 4][:, TOK - s:TOK], z_ps[k % 2][:, 0:s], ACT.Sigmoid, scale=SCALE).then_inc(brk_done, 1)

            def keys_hi(i, m, g):
                gi, c0 = groups_before(m) + g, P if g == 0 else 0
                act.wait_ge(aT_psum, i * (2 * GH) + (gi + 1))
                wait(act, av_done, i * (2 * GH) + groups_before(m - 1))
                act.activation(aT[m % 2][0][:, g * HALF + c0:(g + 1) * HALF], psum[:, 4 + gi % 2, c0:HALF],
                               ACT.Copy).then_inc(aT_hi, 1)

            def out_low(i, r):
                act.wait_ge(av_done, i * (2 * GH) + groups_before(2 * r + 2))
                wait(act, o_add, i * 4 + (r - 1))
                act.activation(o_low[:, r % 2, :], psum[HD:P, 6 + r % 2, :], ACT.Copy).then_inc(o_lo, 1)

            def out_hi(i, r):
                h2, g = r // 2, r % 2
                act.wait_ge(o_add, i * 4 + (r + 1))
                act.wait_ge(o_add, 1)
                act.activation(hT[0][h2 * HD:(h2 + 1) * HD, bass.ds(i, 1), g * HALF:(g + 1) * HALF],
                               o_sum[h2 * HD:(h2 + 1) * HD, g:g + 1, :], ACT.Copy).then_inc(o_hi, 1)

            def att_step(i):
                first, last = isinstance(i, int) and i == 0, isinstance(i, int) and i == HEADS // 2 - 1
                if first:
                    for k in range(2):
                        keep_tile(0, k)
                        break_tile(0, k)
                for m in range(2 * QP):
                    more = not (last and m == 2 * QP - 1)
                    out = None if m % 2 == 0 or (first and m == 1) else (i, m // 2 - 1) if m > 1 else (i - 1, 3)
                    if more:
                        keep_tile(i, 2 * m + 2)
                        break_tile(i, 2 * m + 2)
                    keys_hi(i, m, 0)
                    if out:
                        out_low(*out)
                    if more:
                        keep_tile(i, 2 * m + 3)
                    if m % QP >= 1:
                        keys_hi(i, m, 1)
                    if more:
                        break_tile(i, 2 * m + 3)
                    for g in range(2, m % QP + 1):
                        keys_hi(i, m, g)
                    if out:
                        out_hi(*out)
            iterate(act, HEADS // 2, att_step)
            out_low(HEADS // 2 - 1, 3)
            out_hi(HEADS // 2 - 1, 3)

            for u in range(2, D // UC):
                act.wait_ge(front_psum, FI_O + (u - 1) * NT)
                hi(U_O + u, u % 2)
            boundary(3, U_M1, (front_psum, FI_M1))
            mlp(U_M1, FI_M1, AI_M1, BI_M1, ACT_GAP)
            boundary(4)

        @block.vector
        def _(dve):
            def post_norm(b, t):
                n = NT * (b - 1) + t
                dve.wait_ge(m_rt, n + 1)
                dve.reciprocal(rstd[:, 0, t:t + 1], rt[:, 0, t:t + 1]).then_inc(post, 1)
                dve.wait_ge(post, 3 * n + 1)
                if t == 0:
                    dve.wait_ge(g_in, 16 * (1 + 2 * (b - 1) + 2) if b < 4 else 16 * 8)
                dve.scalar_tensor_tensor(acc[:, t, :], acc[:, t, :], rstd[:, 0, t:t + 1], gpost[:], ALU.mult, ALU.mult).then_inc(post, 1)
                dve.wait_ge(post, 3 * n + 2)
                dve.wait_ge(x_in[t % 4], 16 * (2 * b + t // 4 + 1))
                dve.tensor_tensor(xt[t % 4][:], acc[:, t, :], xt[t % 4][:], ALU.add).then_inc(post, 1)

            def pre_norm(b, t):
                n = NT * b + t
                dve.wait_ge(x_rt, n + 1)
                dve.reciprocal(rstd[:, 1, t:t + 1], rt[:, 1, t:t + 1]).then_inc(pre, 1)
                dve.wait_ge(pre, 2 * n + 1)
                if b == 0 and t == 0:
                    dve.wait_ge(g_in, 16)
                wait(dve, hT_psum, HB * b + 2 * t - 2)
                dve.scalar_tensor_tensor(h_nat[t % 2][:], xt[t % 4][:], rstd[:, 1, t:t + 1], gpre[:], ALU.mult, ALU.mult).then_inc(pre, 1)

            hi_count = [0]

            def take_lo(b, t):
                for q in range(2):
                    hi_count[0] += 1
                    dve.wait_ge(front_hi, hi_count[0])
                    dst = slice(t * P, (t + 1) * P)
                    dve.tensor_tensor(hT[1][:, 4 * q:4 * q + 4, dst], psum[:, 2 + q, :].rearrange("p (k n) -> p k n", k=4),
                                      hT[0][:, 4 * q:4 * q + 4, dst].bitcast(F32), ALU.subtract).then_inc(hT_done, 1)

            def boundary(b, finish):
                for t in range(NT):
                    finish(t)
                    if b < 4 and t >= 1:
                        pre_norm(b, t - 1)
                    post_norm(b, t)
                    if b < 4 and t >= 2:
                        take_lo(b, t - 2)
                if b < 4:
                    pre_norm(b, NT - 1)
                    take_lo(b, NT - 2)
                    take_lo(b, NT - 1)

            for t in range(NT + 1):
                if t < NT:
                    pre_norm(0, t)
                if t:
                    take_lo(0, t - 1)

            for q in range(2):
                dve.wait_ge(ws_hi, q + 1)
                dve.tensor_tensor(wsT[1][:, q * HALF:(q + 1) * HALF], psum[:, 4 + q, :],
                                  wsT[0][:, q * HALF:(q + 1) * HALF].bitcast(F32), ALU.subtract).then_inc(back_evac, 1)
            for q in range(2):
                dve.wait_ge(back_psum, q + 3)
                dve.tensor_copy(rs_bc[:, q * HALF:(q + 1) * HALF], psum[:, 6 + q, :]).then_inc(back_evac, 1)

            with dve.Fori(0, AW // UC // 2) as i:
                for b in range(2):
                    for t in range(NT):
                        dve.wait_ge(act_evac, i * (2 * NT) + (FI_V + b * NT + t + 1))
                        dve.wait_ge(act_evac, FI_V + 1)
                        dve.bn_stats(stats[:, t, bass.ds(2 * i + b, 1), :], vring[:, b, t, :]).then_inc(v_stats, 1)
            dve.wait_ge(v_stats, NT * AW // UC)
            for t in range(NT):
                dve.bn_aggr(mv[:, t, :], stats[:, t].rearrange("p u s -> p (u s)")).then_inc(v_norm, 1)
            dve.wait_ge(v_sqrt, 1)
            dve.reciprocal(v_rs[:], v_rt[:]).then_inc(v_norm, 1)
            dve.wait_ge(v_norm, NT + 1)
            dve.wait_ge(vecs, 48)
            for b in range(2):
                dve.wait_ge(v_out[b], 16 * AW // UC // 2)

            def accumulate(c_first, bi, j, per):
                dve.wait_ge(back_psum, bi + 1)
                dst = acc[:, j // 2, (j % 2) * HALF:(j % 2 + 1) * HALF]
                src = psum[:, 4 + j % 4, :]
                if c_first:
                    return dve.tensor_copy(dst, src)
                dve.wait_ge(back_evac, bi - (per - 1))
                return dve.tensor_tensor(dst, src, dst, ALU.add)

            def gate_chunk(c, ab):
                dve.wait_ge(v_in, c * 16 + 16)
                for t in range(NT):
                    ins = dve.tensor_scalar(vst[:, t, :], vst[:, t, :], mv[:, t, 0:1], v_rs[:, t:t + 1],
                                            ALU.subtract, ALU.mult)
                ins.then_inc(vn_nat, 1)
                wait(dve, gate, c * 4)
                for f in range(2):
                    dve.scalar_tensor_tensor(bb[:, f, :], rs_bc[:, bass.ds(c * P, P)], vb_c[:, bass.ds(c * 2 + f, 1)],
                                             bs_bc[:, bass.ds(c * P, P)], ALU.mult, ALU.add).then_inc(bb_set, 1)
                dve.wait_ge(vn_hi, c + 1)
                dve.tensor_tensor(vn[1][:], vst[:], vn[0][:].bitcast(F32), ALU.subtract).then_inc(vn_lo, 1)
                dve.wait_ge(bb_set, c * 2 + 2)

                def gated_lo(j):
                    dve.wait_ge(ch_hi, c * 4 + (j + 1))
                    dst = (slice(None), j % 2, slice((j // 2) * HALF, (j // 2 + 1) * HALF))
                    dve.tensor_tensor(a_buf[ab][1][dst], ut[:, j, :], a_buf[ab][0][dst].bitcast(F32),
                                      ALU.subtract).then_inc(ch_lo, 1)

                for j in range(4):
                    f = j % 2
                    bi = mix_item(c) + j
                    dve.wait_ge(back_psum, bi + 1)
                    dve.wait_ge(act_evac, c * 4 + (FI_A + j + 1))
                    dve.scalar_tensor_tensor(psum[:, 4 + j, :].rearrange("p (t n) -> p t n", t=4),
                                             psum[:, 4 + j, :].rearrange("p (t n) -> p t n", t=4),
                                             vg_c[:, bass.ds(c * 2 + f, 1)],
                                             bb[:, f:f + 1, :].to_broadcast([P, 4, P]), ALU.mult, ALU.add).then_inc(gate, 1)
                    dve.wait_ge(gate, c * 4 + (j + 1))
                    ins = dve.tensor_tensor(ut[:, j, :], psum[:, 4 + j, :], ut[:, j, :], ALU.mult)
                    ins.then_inc(back_evac, 1)
                    if j:
                        gated_lo(j - 1)
                gated_lo(3)

            def s_part(c, bi0, per, extra, copy):
                for j in range(16):
                    accumulate(copy, c * per + (bi0 + extra + j), j, per).then_inc(back_evac, 1)

            def gate_step(i):
                first = isinstance(i, int) and i == 0
                if first:
                    gate_chunk(0, 0)
                gate_chunk(2 * i + 1, 1)
                if isinstance(i, int) and i == CH_A // 2 - 1:
                    return
                s_part(2 * i, BI_A, 20, 8, first)
                gate_chunk(2 * i + 2, 0)
                s_part(2 * i + 1, BI_A, 20, 8, False)
            iterate(dve, CH_A // 2, gate_step)

            def finish_tail(b):
                bi, per = TAIL[b], 20 if b == 1 else 16

                def finish(t):
                    for n2 in range(2):
                        ins = accumulate(False, bi + 2 * t + n2, 2 * t + n2, per)
                        ins.then_inc(back_evac, 1)
                return finish

            boundary(1, finish_tail(1))

            def mlp(ai0, bi0, r0):
                def chunk(c, ab):
                    for j in range(4):
                        dst = (slice(None), j % 2, slice((j // 2) * HALF, (j // 2 + 1) * HALF))
                        dve.wait_ge(ch_hi, c * 4 + (ai0 + j + 1))
                        dve.tensor_tensor(relu[j % 2][:], relu[j % 2][:], relu[j % 2][:], ALU.mult).then_inc(relu_sq, 1)
                        dve.wait_ge(relu_sq, c * 4 + (r0 + j + 1))
                        dve.tensor_tensor(a_buf[ab][1][dst], relu[j % 2][:], a_buf[ab][0][dst].bitcast(F32),
                                          ALU.subtract).then_inc(ch_lo, 1)

                def step(i):
                    first = isinstance(i, int) and i == 0
                    if first:
                        chunk(0, 0)
                    chunk(2 * i + 1, 1)
                    if isinstance(i, int) and i == CH_M // 2 - 1:
                        return
                    s_part(2 * i, bi0, 16, 0, first)
                    chunk(2 * i + 2, 0)
                    s_part(2 * i + 1, bi0, 16, 0, False)
                iterate(dve, CH_M // 2, step)

            mlp(AI_M0, BI_M0, 0)
            boundary(2, finish_tail(2))

            for u in range(D // UC):
                b = u % 2
                for t in range(NT):
                    hi_count[0] += 1
                    dve.wait_ge(front_hi, hi_count[0])
                    dve.tensor_tensor(v2ring[b][:, :, t, 1, :],
                                      psum[:, t % (4 if u else 2), 0:UC].rearrange("p (h d) -> p h d", h=4),
                                      v2ring[b][:, :, t, 0, :].bitcast(F32), ALU.subtract).then_inc(dve_evac, 1)
            with dve.Fori(0, D // UC) as i:
                for b in range(2):
                    for j in range(4):
                        dst = (slice(None), j % 2, slice((j // 2) * HALF, (j // 2 + 1) * HALF))
                        dve.wait_ge(front_hi, i * 8 + (hi_count[0] + 4 * b + j + 1))
                        ins = dve.tensor_tensor(a_buf[b][1][dst], psum[:, j, :], a_buf[b][0][dst].bitcast(F32), ALU.subtract)
                        ins.then_inc(dve_evac, 1)
            hi_count[0] += 4 * 2 * D // UC

            dve.wait_ge(x_out, 16 * NT * 2)
            for b in range(2):
                for s in range(2):
                    dve.memset(aT[b][s][:, 0:P].bitcast(F32), 0.0).then_inc(rows_set, 1)
            for b in range(2):
                dve.wait_ge(qk_out[b], 32 * (2 * D // UC) // 2)
            for b in range(4):
                dve.memset(stick[b][:, TOK:TOK + 1], 1.0).then_inc(rows_set, 1)
            dve.wait_ge(rows_set, 8)

            def sticks(i, k):
                s = (k % NT + 1) * P
                dve.wait_ge(keep_done, i * (2 * NT) + (k + 1))
                row = stick[k % 4][:, TOK - s:TOK][:, ::-1]
                dve.tensor_tensor_scan(row, row, row, 1.0, ALU.mult, ALU.bypass).then_inc(stick_done, 1)

            def keys_lo(i, m, g):
                gi, c0 = groups_before(m) + g, P if g == 0 else 0
                dst = (slice(None), slice(g * HALF + c0, (g + 1) * HALF))
                dve.wait_ge(aT_hi, i * (2 * GH) + (gi + 1))
                dve.tensor_tensor(aT[m % 2][1][dst], psum[:, 4 + gi % 2, c0:HALF],
                                  aT[m % 2][0][dst].bitcast(F32), ALU.subtract).then_inc(aT_lo, 1)

            def out_sum(i, r):
                h2, g = r // 2, r % 2
                half = slice(h2 * HD, (h2 + 1) * HD)
                dve.wait_ge(o_lo, i * 4 + (r + 1))
                wait(dve, o_split, i * 4 + (r - 1))
                dve.tensor_tensor(o_sum[half, g, :], psum[0:HD, 6 + g, :], o_low[:, g, :], ALU.add).then_inc(o_add, 1)

            def out_lo(i, r):
                h2, g = r // 2, r % 2
                half = slice(h2 * HD, (h2 + 1) * HD)
                dve.wait_ge(o_hi, i * 4 + (r + 1))
                dst = (half, bass.ds(i, 1), slice(g * HALF, (g + 1) * HALF))
                dve.tensor_tensor(hT[1][dst], o_sum[half, g:g + 1, :], hT[0][dst].bitcast(F32),
                                  ALU.subtract).then_inc(o_split, 1)

            def att_step(i):
                first, last = isinstance(i, int) and i == 0, isinstance(i, int) and i == HEADS // 2 - 1
                if first:
                    sticks(0, 0)
                    sticks(0, 1)
                for m in range(2 * QP):
                    more = not (last and m == 2 * QP - 1)
                    out = None if m % 2 == 0 or (first and m == 1) else (i, m // 2 - 1) if m > 1 else (i - 1, 3)
                    if more:
                        sticks(i, 2 * m + 2)
                    keys_lo(i, m, 0)
                    if out:
                        out_sum(*out)
                    if more:
                        sticks(i, 2 * m + 3)
                    for g in range(1, m % QP + 1):
                        keys_lo(i, m, g)
                    if out:
                        out_lo(*out)
            iterate(dve, HEADS // 2, att_step)
            out_sum(HEADS // 2 - 1, 3)
            out_lo(HEADS // 2 - 1, 3)

            def o_part(u, t):
                bank = t % (4 if u < D // UC - 1 else 2)
                dve.wait_ge(front_psum, FI_O + u * NT + t + 1)
                if u == 0 and t == 0:
                    dve.wait_ge(av_done, GH * HEADS)
                return dve.tensor_copy(acc[:, t, u * UC:(u + 1) * UC], psum[:, bank, 0:UC])

            for u in range(D // UC - 1):
                for t in range(NT):
                    o_part(u, t).then_inc(dve_evac, 1)

            def o_finish(t):
                o_part(D // UC - 1, t).then_inc(dve_evac, 1)
            boundary(3, o_finish)
            mlp(AI_M1, BI_M1, 4 * CH_M)
            boundary(4, finish_tail(4))


TAIL = {1: BI_A + 20 * (CH_A - 2) + 8, 2: BI_M0 + 16 * (CH_M - 2), 4: BI_M1 + 16 * (CH_M - 2)}


INPUTS = ["x", "norm_mix_pre", "norm_mix_post", "norm_ffn_pre", "norm_ffn_post", "a_w_in", "a_v_g", "a_v_b",
          "a_w_s", "a_b_s", "a_w_out", "b_w_qkv", "b_w_out", "mlp_w1", "mlp_w2"]


def kernel(**inputs):
    import numpy as np
    import concourse.bacc as bacc
    from concourse.bass_utils import run_bass_kernel_spmd

    nc = bacc.Bacc("TRN2", target_bir_lowering=False, num_devices=1, dynamic_dma_scratch_size=1024)
    arrays, ap = {}, {}
    for name in INPUTS:
        a = np.ascontiguousarray(inputs[name])
        arrays[name + "_in"] = a
        ap[name] = nc.dram_tensor(name + "_in", a.shape, F32, kind="ExternalInput").ap()
    y = nc.dram_tensor("y_out", (TOK, D), F32, kind="ExternalOutput").ap()
    build(nc, ap["x"][0], ap["norm_mix_pre"], ap["norm_mix_post"], ap["norm_ffn_pre"], ap["norm_ffn_post"],
          ap["a_w_in"][0], ap["a_v_g"], ap["a_v_b"], ap["a_w_s"][0], ap["a_b_s"][0], ap["a_w_out"][0],
          ap["b_w_qkv"][0], ap["b_w_out"][0], ap["mlp_w1"], ap["mlp_w2"], y)
    r = run_bass_kernel_spmd(nc, [arrays], core_ids=[0])
    return r.results[0]["y_out"].reshape(1, TOK, D)
```

```python
from contextlib import ExitStack

import concourse.bass as bass
import concourse.mybir as mybir
from concourse.alu_op_type import AluOpType as ALU

F32, F32R, BF16 = mybir.dt.float32, mybir.dt.float32r, mybir.dt.bfloat16
ACT = mybir.ActivationFunctionType

P = 128
D = 1024
TOK = 1024
NT = TOK // P
KT = D // P
FF = 4 * D
AW = 2 * D
GROUPS = 8
UC = 256
US = KT * UC
HALF = 512
HEADS, HD = 16, 64
EPS = 1e-6
SCALE = HD ** -0.5
MASKED = -1.0e30
PASSES = ((0, 0), (0, 1), (1, 0))

CH_A, CH_M = AW // UC, FF // UC
U_V = 0
U_A = U_V + AW // UC
U_M0 = U_A + 2 * CH_A
U_V2 = U_M0 + 2 * CH_M
U_QK = U_V2 + D // UC
U_O = U_QK + 2 * D // UC
U_M1 = U_O + D // UC
U_END = U_M1 + 2 * CH_M

FI_V = 0
FI_A = FI_V + NT * AW // UC
FI_M0 = FI_A + 4 * CH_A
FI_V2 = FI_M0 + 4 * CH_M
FI_QK = FI_V2 + NT * D // UC
FI_O = FI_QK + 4 * 2 * D // UC
FI_M1 = FI_O + NT * D // UC
ACT_GAP = FI_M1 - FI_V2
V2_FIRST = (0, 1, 6, 7, 4, 5, 0, 1)
HB = 2 * NT

BI_SET = 0
BI_A = BI_SET + 4
BI_M0 = BI_A + 4 * CH_A + 16 * (CH_A - 1)
BI_M1 = BI_M0 + 16 * (CH_M - 1)

AI_A, AI_M0, AI_M1 = 0, 4 * CH_A, 4 * CH_A + 4 * CH_M


def wait(eng, sem, value):
    if isinstance(value, int) and value <= 0:
        return
    eng.wait_ge(sem, value)


def post_steps(b, t):
    return (2 * NT + 2) * (b - 1) + 2 * (t + 1) + max(0, t - 5)


def hT_bank(b, t):
    return 4 if b and t == NT - 2 else 2


def x_steps(b, t):
    return 6 * (b - 1) + t + 1


def iterate(eng, n, emit):
    emit(0)
    if n > 2:
        with eng.Fori(1, n - 1) as i:
            emit(i)
    if n > 1:
        emit(n - 1)


def mix_item(c):
    return BI_A if isinstance(c, int) and c == 0 else c * 20 + (BI_A - 16)


def s_end(c, bi0, per, extra):
    return bi0 if isinstance(c, int) and c < 0 else c * per + (bi0 + extra + 16)


QP = NT // 2
GH = QP * (QP + 1) // 2
ORDER = (0, 1, 3, 2)


def pair(n):
    return ORDER[n % QP]


def groups_before(n):
    return (n // QP) * GH + sum(m + 1 for m in ORDER[:n % QP])


def tile_of(k):
    m, e = pair(k // 2), k % 2
    return (k // NT) % 2, m, e, 2 * m + e


def build(nc, x, g_mix_pre, g_mix_post, g_ffn_pre, g_ffn_post, w_in, v_g, v_b, w_s, b_s, w_aout,
          w_qkv, w_bout, w1, w2, out):
    ctx = ExitStack()
    with ctx:
        def sem(name):
            return ctx.enter_context(nc.semaphore(name))

        place = [-(-nc.sbuf_base // 64) * 64]

        def at(name, shape, dt, offset=None):
            size = 4 if dt != BF16 else 2
            for s in shape[1:]:
                size *= s
            if offset is None:
                offset = place[0]
                place[0] += -(-size // 32) * 32
                assert place[0] <= 229344, (name, place[0])
            return nc.alloc_sbuf_tensor_at(name, shape, dt, offset=offset)

        hT = [at("hT_hi", [P, KT, TOK], F32R), at("hT_lo", [P, KT, TOK], F32R)]
        o_acc = place[0]
        acc = at("acc", [P, NT, D], F32)
        o_a = place[0]
        a_buf = [[at(f"a{b}_{s}", [P, 2, TOK], F32R) for s in ("hi", "lo")] for b in range(2)]
        stage = at("stage", [P, US], F32)
        wt = [[at(f"w{b}_{s}", [P, US], F32R) for s in ("hi", "lo")] for b in range(2)]
        vring = at("vring", [P, 2, NT, UC], F32, o_acc)
        v2ring = [at(f"v2ring{b}", [P, 4, NT, 2, HD], F32R, o_acc + b * 16384) for b in range(2)]
        q_st = [at(f"q_st{b}", [P, TOK], F32R, o_acc + b * 16384) for b in range(2)]
        k_st = [[at(f"k_st{b}{s}", [P, TOK], F32R, o_acc + b * 16384 + 4096 * (s + 1)) for s in range(2)]
                for b in range(2)]
        v_st = [at(f"v_st{b}", [P, NT, 2 * HD], F32R, o_acc + b * 16384 + 12288) for b in range(2)]
        o_brk = [o_a + m * (m + 1) * 1024 for m in range(3)] + [o_a + 16384 - P * 4]
        brk = [[at(f"brk{m}{e}", [P, (2 * m + 2) * P], F32, o_brk[m] + e * (m + 1) * 1024)
                for e in range(2)] for m in range(QP)]
        ws_nat = at("ws_nat", [P, GROUPS, P], F32, o_a)
        o_const = place[0]
        wsT = at("wsT", [P, GROUPS, 2, P], F32R)
        rs_bc = at("rs_bc", [P, GROUPS * P], F32)
        bs_bc = at("bs_bc", [P, GROUPS * P], F32)
        relu = [at(f"relu{b}", [P, HALF], F32, o_const + b * 2048) for b in range(2)]
        o_low = at("o_low", [HD, 2, HALF], F32, o_const)
        o_sum = at("o_sum", [P, 2, HALF], F32, o_const + 4096)
        o_scr = place[0]
        xt = [at(f"xt{b}", [P, D], F32) for b in range(4)]
        gpost = at("gpost", [P, D], F32)
        gpre = at("gpre", [P, D], F32)
        h_nat = [at(f"h_nat{b}", [P, D], F32) for b in range(2)]
        junk = at("junk", [P, D], BF16)
        vst = at("vst", [P, NT, UC], F32, o_scr)
        vn = [at("vn_hi", [P, NT, UC], F32R, o_scr + 8192), at("vn_lo", [P, NT, UC], F32R, o_scr + 16384)]
        ut = at("ut", [P, 4, HALF], F32, o_scr + 24576)
        bb = at("bb", [P, 2, P], F32, o_scr + 32768)
        aT = [[at(f"aT{q}_{s}", [P, (4 - q) * HALF], F32R, o_scr + q * 16384 + n * (4 - q) * 2048)
               for n, s in enumerate(("hi", "lo"))] for q in range(2)]
        o_stick = {0: o_a + 12288, 1: o_scr + 28672, 2: o_const + 8192, 3: o_a + 16384 - P * 4 + 8192}
        stick = [[at(f"stick{m}{e}", [P, (2 * m + 2) * P + 8], F32, o_stick[m] + e * ((m + 1) * 1024 + 32))
                  for e in range(2)] for m in range(QP)]
        ident = at("ident", [P, P], F32)
        ident_bf = at("ident_bf", [P, P], BF16)
        mask_bf = at("mask_bf", [P, P], BF16)
        ones = at("ones", [P, P], F32R)
        eps = at("eps", [P, 1], F32)
        o_mix = place[0]
        mix_lo = at("mix_lo", [P, 4, P], F32)
        stats = at("stats", [P, NT, AW // UC, 6], F32, o_mix)
        mv = at("mv", [P, NT, 2], F32)
        v_rt = at("v_rt", [P, NT], F32)
        v_rs = at("v_rs", [P, NT], F32)
        vg_c = at("vg_c", [P, AW // P], F32)
        vb_c = at("vb_c", [P, AW // P], F32)
        ss = at("ss", [P, 2, NT], F32)
        rt = at("rt", [P, 2, NT], F32)
        rstd = at("rstd", [P, 2, NT], F32)

        psum = ctx.enter_context(nc.psum_tensor("psum", [P, 8, HALF], F32))
        z_ps = [psum[:, 2 * b:2 * b + 2, :].rearrange("p a n -> p (a n)") for b in range(2)]

        xres = [nc.dram_tensor(f"x_res{n}", (TOK, D), F32, kind="Internal").ap() for n in range(3)]
        v_dram = nc.dram_tensor("v_gelu", (AW // UC, P, NT * UC), F32, kind="Internal").ap()
        qk_dram = [nc.dram_tensor(f"qk_{s}", (2 * D, TOK), F32R, kind="Internal").ap() for s in ("hi", "lo")]
        v2_dram = nc.dram_tensor("v_heads", (HEADS, P, NT * 2 * HD), F32R, kind="Internal").ap()

        def rows(ap):
            return ap.rearrange("(t p) n -> t p n", p=P)

        x_from = [rows(x), rows(x), rows(xres[0]), rows(xres[1]), rows(xres[2])]
        x_to = [None, rows(xres[0]), rows(xres[1]), rows(xres[2]), rows(out)]

        unit_landed = sem("unit_landed")
        unit_hi = sem("unit_hi")
        unit_ready = sem("unit_ready")
        front_psum = sem("front_psum")
        act_evac = sem("act_evac")
        dve_evac = sem("dve_evac")
        front_hi = sem("front_hi")
        hT_psum = sem("hT_psum")
        hT_done = sem("hT_done")
        back_psum = sem("back_psum")
        back_evac = sem("back_evac")
        tail_first = sem("tail_first")
        ch_hi = sem("ch_hi")
        ch_lo = sem("ch_lo")
        relu_sq = sem("relu_sq")
        consts = sem("consts")
        eps_set = sem("eps_set")
        vecs = sem("vecs")
        ws_in = sem("ws_in")
        ws_masked = sem("ws_masked")
        ws_hi = sem("ws_hi")
        x_in = [sem(f"x_in{b}") for b in range(4)]
        g_in = sem("g_in")
        x_out = sem("x_out")
        m_sq = sem("m_sq")
        m_rt = sem("m_rt")
        post = sem("post")
        x_add = sem("x_add")
        x_sq = sem("x_sq")
        x_rt = sem("x_rt")
        pre = sem("pre")
        v_stats = sem("v_stats")
        v_out = [sem(f"v_out{b}") for b in range(2)]
        v_norm = sem("v_norm")
        v_sqrt = sem("v_sqrt")
        v_in = sem("v_in")
        vn_nat = sem("vn_nat")
        vn_hi = sem("vn_hi")
        vn_lo = sem("vn_lo")
        bb_set = sem("bb_set")
        gate = sem("gate")
        qk_out = [sem(f"qk_out{b}") for b in range(2)]
        v2_out = [sem(f"v2_out{b}") for b in range(2)]
        qk_in = [sem(f"qk_in{b}") for b in range(2)]
        vh_in = [sem(f"vh_in{b}") for b in range(2)]
        z_done = sem("z_done")
        keep_done = sem("keep_done")
        brk_done = sem("brk_done")
        rows_set = sem("rows_set")
        stick_done = sem("stick_done")
        a_done = sem("a_done")
        aT_psum = sem("aT_psum")
        aT_hi = sem("aT_hi")
        aT_lo = sem("aT_lo")
        av_done = sem("av_done")
        o_lo = sem("o_lo")
        o_add = sem("o_add")
        o_hi = sem("o_hi")
        o_split = sem("o_split")

        block = ctx.enter_context(nc.Block())

        def cols(w, c):
            return w.rearrange("(k p) f -> p k f", p=P)[:, :, bass.ds(c * UC, UC)]

        def rws(w, c):
            return w.rearrange("(r p) n -> p r n", p=P)[:, bass.ds(c * 2, 2), :]

        def x_new(eng, b, t):
            if t < 6:
                eng.wait_ge(x_add, x_steps(b, t))
            else:
                eng.wait_ge(post, post_steps(b, t))

        stage_c = stage[:].rearrange("p (k f) -> p k f", k=KT)
        stage_r = stage[:].rearrange("p (r n) -> p r n", r=2)

        @block.sync
        def _(sp):
            def unit(n, src, dst):
                wait(sp, unit_ready, n * 2)
                sp.dma_start(dst, src).then_inc(unit_landed, 16)

            def load_x(b, t):
                if t >= 4:
                    if b < 4:
                        sp.wait_ge(pre, 2 * (NT * b + t - 3))
                    if b:
                        sp.wait_ge(x_out, 16 * (NT * (b - 1) + t - 3))
                elif t == 0:
                    wait(sp, pre, 2 * NT * b)
                    wait(sp, x_out, 16 * NT * (b - 1))
                sp.dma_start(xt[t % 4][:], x_from[b][t]).then_inc(x_in[t % 4], 16)

            def load_g(b):
                wait(sp, pre, 2 * NT * min(b, 4))
                if b:
                    g = (g_mix_post, g_ffn_post)[(b - 1) % 2][(b - 1) // 2:(b - 1) // 2 + 1, :]
                    sp.dma_start(gpost[:], g.to_broadcast([P, D])).then_inc(g_in, 16)
                if b < 4:
                    g = (g_mix_pre, g_ffn_pre)[b % 2][b // 2:b // 2 + 1, :]
                    sp.dma_start(gpre[:], g.to_broadcast([P, D])).then_inc(g_in, 16)

            def boundary(b):
                for t in range(NT):
                    if b:
                        x_new(sp, b, t)
                        sp.dma_start(x_to[b][t], xt[t % 4][:]).then_inc(x_out, 16)
                    if t + 4 < NT:
                        load_x(b, t + 4)

            def gmlp_units():
                def up(c):
                    unit(U_A + 2 * c - (0 if isinstance(c, int) and c == 0 else 1), cols(w_in, c), stage_c)

                def load_v(c):
                    wait(sp, vn_lo, c)
                    if isinstance(c, int) and c == 0:
                        for b in range(2):
                            wait(sp, v_out[b], 16 * AW // UC // 2)
                        wait(sp, pre, 2 * NT)
                        wait(sp, hT_psum, HB)
                    sp.dma_start(vst[:].rearrange("p t f -> p (t f)"),
                                 v_dram[bass.ds(c, 1)].rearrange("o p f -> (o p) f")).then_inc(v_in, 16)

                def step(i):
                    if isinstance(i, int) and i == 0:
                        up(0)
                        up(1)
                        load_v(0)
                    else:
                        up(2 * i + 1)
                    load_v(2 * i + 1)
                    unit(U_A + 2 + 4 * i, rws(w_aout, 2 * i), stage_r)
                    if not (isinstance(i, int) and i == CH_A // 2 - 1):
                        up(2 * i + 2)
                        load_v(2 * i + 2)
                        unit(U_A + 4 + 4 * i, rws(w_aout, 2 * i + 1), stage_r)
                iterate(sp, CH_A // 2, step)
                unit(U_A + 2 * CH_A - 1, rws(w_aout, CH_A - 1), stage_r)

            load_x(0, 0)
            load_g(0)
            load_x(0, 1)
            unit(U_V, cols(w_in, AW // UC), stage_c)
            for t in range(2, 4):
                load_x(0, t)
            boundary(0)
            unit(U_V + 1, cols(w_in, AW // UC + 1), stage_c)
            sp.dma_start(ws_nat[:], w_s.rearrange("g t s -> t g s")).then_inc(ws_in, 16)
            sp.dma_start(bs_bc[:], b_s.rearrange("(o g) t -> o (g t)", o=1).to_broadcast([P, GROUPS * P])).then_inc(vecs, 16)
            with nc.allow_non_contiguous_dma("two vectors of 2048 values"):
                sp.dma_start(vg_c[:], v_g.rearrange("o (c p) -> p (o c)", p=P)).then_inc(vecs, 16)
                sp.dma_start(vb_c[:], v_b.rearrange("o (c p) -> p (o c)", p=P)).then_inc(vecs, 16)

            with sp.Fori(2, AW // UC) as u:
                unit(U_V + u, cols(w_in, u + AW // UC), stage_c)
            gmlp_units()
            wait(sp, ch_lo, AI_A + 4 * CH_A)
            for t in range(4):
                load_x(1, t)
            load_g(1)
            unit(U_M0, cols(w1[0], 0), stage_c)
            boundary(1)

            def mlp_rest(u0, layer):
                def load_up(c):
                    unit(u0 + 2 * c - 1, cols(w1[layer], c), stage_c)

                def step(i):
                    load_up(2 * i + 1)
                    unit(u0 + 2 + 4 * i, rws(w2[layer], 2 * i), stage_r)
                    if not (isinstance(i, int) and i == CH_M // 2 - 1):
                        load_up(2 * i + 2)
                        unit(u0 + 4 + 4 * i, rws(w2[layer], 2 * i + 1), stage_r)
                iterate(sp, CH_M // 2, step)

            mlp_rest(U_M0, 0)
            load_g(2)
            for t in range(4):
                load_x(2, t)
            unit(U_V2 - 1, rws(w2[0], CH_M - 1), stage_r)
            unit(U_V2, cols(w_qkv, 2 * D // UC), stage_c)
            boundary(2)
            with sp.Fori(1, D // UC) as u:
                unit(U_V2 + u, cols(w_qkv, u + 2 * D // UC), stage_c)
            with sp.Fori(0, 2 * D // UC) as u:
                unit(U_QK + u, cols(w_qkv, u), stage_c)
            unit(U_O, cols(w_bout, 0), stage_c)

            def load_qk(h, b):
                wait(sp, z_done, h * NT - NT)
                for s in range(2):
                    r = slice(s * HD, (s + 1) * HD)
                    sp.dma_start(q_st[b][r, :].bitcast(F32), qk_dram[s][bass.ds(h * HD, HD), :].bitcast(F32)).then_inc(qk_in[b], 16)
                    for s2 in range(2):
                        sp.dma_start(k_st[b][s2][r, :].bitcast(F32), qk_dram[s2][bass.ds(h * HD + D, HD), :].bitcast(F32)).then_inc(qk_in[b], 16)

            def load_v(h, b):
                wait(sp, av_done, h * GH - GH)
                sp.dma_start(v_st[b][:].rearrange("p t d -> p (t d)").bitcast(F32),
                             v2_dram[bass.ds(h, 1)].rearrange("o p f -> (o p) f").bitcast(F32)).then_inc(vh_in[b], 16)

            for b in range(2):
                wait(sp, v2_out[b], 64 * (D // UC) // 2)
            wait(sp, qk_out[0], 32 * ((D // UC) // 2 + 1))
            for h in range(2):
                load_qk(h, h)
                load_v(h, h)
            unit(U_O + 1, cols(w_bout, 1), stage_c)
            for b in range(2):
                wait(sp, qk_out[b], 32 * (2 * D // UC) // 2)
            unit(U_O + 2, cols(w_bout, 2), stage_c)
            with sp.Fori(1, HEADS // 2) as i:
                for b in range(2):
                    load_qk(2 * i + b, b)
                    load_v(2 * i + b, b)
            wait(sp, o_split, 2 * HEADS)
            load_g(3)
            for t in range(4):
                load_x(3, t)
            unit(U_O + 3, cols(w_bout, 3), stage_c)
            unit(U_M1, cols(w1[1], 0), stage_c)
            boundary(3)
            mlp_rest(U_M1, 1)
            load_g(4)
            for t in range(4):
                load_x(4, t)
            unit(U_END - 1, rws(w2[1], CH_M - 1), stage_r)
            boundary(4)
            wait(sp, x_out, 16 * NT * 4)

        @block.gpsimd
        def _(pool):
            pool.memset(eps[:], EPS).then_inc(eps_set, 1)
            pool.memset(ident[:], 0.0).then_inc(consts, 1)
            pool.memset(mask_bf[:], 0.0).then_inc(consts, 1)
            pool.memset(ones[:].bitcast(F32), 1.0).then_inc(consts, 1)
            pool.wait_ge(consts, 2)
            pool.affine_select(out=ident[:], in_=ident[:], compare_op=ALU.not_equal, fill=1.0, base=0,
                               pattern=[[-1, P]], channel_multiplier=1).then_inc(consts, 1)
            pool.affine_select(out=mask_bf[:], in_=mask_bf[:], compare_op=ALU.is_gt, fill=MASKED, base=0,
                               pattern=[[-1, P]], channel_multiplier=1).then_inc(consts, 1)
            pool.wait_ge(eps_set, 1)
            pool.wait_ge(consts, 4)
            pool.tensor_copy(ident_bf[:], ident[:]).then_inc(consts, 1)

            def lo(n, b):
                pool.wait_ge(unit_hi, n + 1)
                for c in (slice(0, US // 2), slice(US // 2, US)):
                    pool.tensor_tensor(wt[b][1][:, c], stage[:, c], wt[b][0][:, c].bitcast(F32),
                                       ALU.subtract).then_inc(unit_ready, 1)

            lo(0, 0)
            pool.wait_ge(ws_in, 16)
            pool.affine_select(out=ws_nat[:], in_=ws_nat[:], compare_op=ALU.is_ge, fill=0.0, base=0,
                               pattern=[[0, GROUPS], [-1, P]], channel_multiplier=1).then_inc(ws_masked, 1)
            lo(1, 1)

            def add_x(b):
                for t in range(6):
                    pool.wait_ge(post, post_steps(b, t))
                    pool.wait_ge(x_in[t % 4], 16 * (2 * b + t // 4 + 1))
                    pool.tensor_tensor(xt[t % 4][:], acc[:, t, :], xt[t % 4][:], ALU.add).then_inc(x_add, 1)

            def lo_units(u0, u1):
                with pool.Fori(u0 // 2, u1 // 2) as i:
                    lo(2 * i, 0)
                    lo(2 * i + 1, 1)

            lo_units(U_V + 2, U_M0)
            add_x(1)
            lo_units(U_M0, U_V2)
            add_x(2)
            lo_units(U_V2, U_O + 2)

            def stick_mult(k, r):
                _, m, e, tb = tile_of(k)
                c0, c1 = (1 - e) * P, (2 * m + 2) * P
                pool.wait_ge(brk_done, r + k + 1)
                pool.wait_ge(stick_done, r + k + 1)
                pool.tensor_tensor(brk[m][e][:, c0:c1], brk[m][e][:, c0:c1], stick[m][e][:, c0 + 1:c1 + 1],
                                   ALU.mult).then_inc(a_done, 1)

            with pool.Fori(0, HEADS // 2) as i:
                for k in range(2 * NT):
                    stick_mult(k, i * (2 * NT))
            for n in range(U_O + 2, U_M1 + 1):
                lo(n, n % 2)
            add_x(3)
            lo(U_M1 + 1, 1)
            lo_units(U_M1 + 2, U_END)
            add_x(4)

        @block.tensor
        def _(pe):
            def t_item(evac, fi, bank, ub, f, half, halves_of=None):
                wait(pe, evac[0], fi - (3 + evac[1]))
                n = 0
                for k in range(KT):
                    if halves_of is not None and k in (0, KT // 2):
                        pe.wait_ge(unit_ready, halves_of * 2 + (1 if k == 0 else 2))
                    for sw, sh in PASSES:
                        mm = pe.matmul(psum[:, bank, :], wt[ub][sw][:, k * UC + f * P:k * UC + (f + 1) * P],
                                       hT[sh][:, k, half * HALF:(half + 1) * HALF],
                                       start=(n == 0), stop=(n == 3 * KT - 1))
                        n += 1
                return mm

            def n_item(evac, fi, bank, ub, t, before=3, c0=0):
                if before is not None:
                    wait(pe, evac[0], fi - (before + evac[1]))
                n = 0
                for k in range(KT):
                    for sh, sw in PASSES:
                        mm = pe.matmul(psum[:, bank, c0:c0 + UC], hT[sh][:, k, t * P:(t + 1) * P],
                                       wt[ub][sw][:, k * UC:(k + 1) * UC],
                                       start=(n == 0), stop=(n == 3 * KT - 1))
                        n += 1
                return mm

            def s_chunk(j, ab, ub, start=True, stop=True):
                t, n2 = j // 2, j % 2
                for n in range(6):
                    r, (sa, sw) = n // 3, PASSES[n % 3]
                    mm = pe.matmul(psum[:, 4 + j % 4, :], a_buf[ab][sa][:, r, t * P:(t + 1) * P],
                                   wt[ub][sw][:, r * D + n2 * HALF:r * D + (n2 + 1) * HALF],
                                   start=(start and n == 0), stop=(stop and n == 5))
                return mm

            def transposes(b, t):
                pe.wait_ge(pre, 2 * (NT * b + t + 1))
                for q in range(2):
                    if hT_bank(b, t) == 2:
                        wait(pe, hT_done, HB * b + 2 * t + q - (3 if b and t == NT - 1 else 1))
                    for j in range(4):
                        k = 4 * q + j
                        mm = pe.transpose(psum[:, hT_bank(b, t) + q, j * P:(j + 1) * P], h_nat[t % 2][:, k * P:(k + 1) * P], ident[:])
                    mm.then_inc(hT_psum, 1)

            def ready(n):
                pe.wait_ge(unit_ready, n * 2 + 2)

            ACT_EV, DVE_EV = (act_evac, 0), (dve_evac, FI_V2)

            pe.wait_ge(consts, 6)
            for t in range(NT // 2):
                transposes(0, t)
            ready(U_V)
            for t in range(NT):
                pe.wait_ge(hT_done, 2 * t + 2)
                n_item(ACT_EV, FI_V + t, 4 + t // 2, 0, t, None, (t % 2) * UC).then_inc(front_psum, 1)
                if t + NT // 2 < NT:
                    transposes(0, t + NT // 2)

            ready(U_V + 1)
            for t in range(NT):
                n_item(ACT_EV, FI_V + NT + t, t % 4, 1, t, None if t < 4 else 3).then_inc(front_psum, 1)
                if t == 3:
                    pe.wait_ge(ws_masked, 1)
                    pe.wait_ge(act_evac, FI_V + NT)
                    for q in range(2):
                        for j in range(4):
                            mm = pe.transpose(psum[:, 4 + q, j * P:(j + 1) * P], ws_nat[:, 4 * q + j, :], ident[:])
                        mm.then_inc(back_psum, 1)
            for q in range(2):
                pe.wait_ge(back_evac, q + 1)
                for s in range(2):
                    mm = pe.matmul(psum[:, 6 + q, :], ones[:], wsT[:, 4 * q:4 * q + 4, s, :],
                                   start=(s == 0), stop=(s == 1))
                mm.then_inc(back_psum, 1)

            def n_units(evac, u0, fi0, i):
                for b in range(2):
                    ready(i * 2 + (u0 + b))
                    for t in range(NT):
                        n_item(evac, i * (2 * NT) + (fi0 + NT * b + t), t % 4, b, t).then_inc(front_psum, 1)

            with pe.Fori(1, AW // UC // 2) as i:
                n_units(ACT_EV, U_V, FI_V, i)

            def chunk_phase(u0, fi0, bi0, ai0, c_n, mix, tail, norm=None, gap=0):
                per = 20 if mix else 16

                def mixing(c, j):
                    half, f = j // 2, j % 2
                    bi = mix_item(c) + j
                    if j == 0:
                        pe.wait_ge(vn_lo, c + 1)
                    pe.wait_ge(back_evac, bi - 1)
                    for t in range(4 * half, 4 * half + 4):
                        bank, c0 = 4 + 2 * (j % 2) + (t % 4) // 2, (t % 2) * 2 * P
                        for sv in range(2):
                            mm = pe.matmul(psum[:, bank, c0:c0 + 2 * P], vn[sv][:, t, f * P:(f + 1) * P],
                                           wsT[:, bass.ds(c, 1)].rearrange("p g s n -> p (g s n)"),
                                           start=(sv == 0), stop=(sv == 1))
                    mm.then_inc(back_psum, 1)

                def up(c, first=False):
                    if not (first and norm is not None):
                        ready(u0 + 2 * c - (0 if first else 1))
                    if first and norm is not None:
                        pe.wait_ge(hT_done, HB * norm + NT)
                    for half in range(2):
                        if first and norm is not None and half:
                            pe.wait_ge(hT_done, HB * (norm + 1))
                        for f in range(2):
                            j = 2 * half + f
                            t_item((act_evac, gap), c * 4 + (fi0 + j), j, 0 if first else 1, f, half,
                                   u0 if first and norm is not None and j == 0 else None).then_inc(front_psum, 1)
                            if mix:
                                for item in (((), (), (0, 1), (2, 3)) if first else ((), (0, 1), (2,), (3,)))[j]:
                                    mixing(c, item)
                            if first and norm is not None and j == 0:
                                pe.wait_ge(back_evac, bi0)
                                for t in range(NT - 3, NT):
                                    transposes(norm, t)

                def behind_mix(j):
                    return {0: 1, 1: 2, 2: 2}.get(j, 3) if mix else 3

                def down(c, ab):
                    ready(u0 + 2 * c + 2)
                    pe.wait_ge(ch_lo, c * 4 + (ai0 + 4))
                    for j in range(16):
                        wait(pe, back_evac, c * per + (bi0 + j + (8 if mix else 0)) - behind_mix(j))
                        s_chunk(j, ab, 0).then_inc(back_psum, 1)

                def step(i):
                    if isinstance(i, int) and i == 0:
                        up(0, first=True)
                    up(2 * i + 1)
                    if isinstance(i, int) and i == c_n // 2 - 1:
                        return
                    down(2 * i, 0)
                    up(2 * i + 2)
                    down(2 * i + 1, 1)
                iterate(pe, c_n // 2, step)

                c = c_n - 2

                def first_chunk(j):
                    wait(pe, back_evac, c * per + (bi0 + j + (8 if mix else 0)) - behind_mix(j))
                    return s_chunk(j, 0, 0, stop=False)

                def second_chunk(j):
                    s_chunk(j, 1, 1, start=False).then_inc(back_psum, 1)

                ready(u0 + 2 * c + 2)
                pe.wait_ge(ch_lo, ai0 + 4 * c_n - 4)
                for j in range(4):
                    first_chunk(j)
                ready(u0 + 2 * c + 3)
                pe.wait_ge(ch_lo, ai0 + 4 * c_n)
                for j in range(4):
                    second_chunk(j)
                for t in range(2, NT - 1):
                    for j in (2 * t, 2 * t + 1):
                        first_chunk(j)
                        second_chunk(j)
                    if tail is not None and t >= 3:
                        transposes(tail, t - 3)
                first_chunk(2 * NT - 2)
                first_chunk(2 * NT - 1).then_inc(tail_first, 1)
                second_chunk(2 * NT - 2)
                second_chunk(2 * NT - 1)
                if tail is not None:
                    transposes(tail, NT - 4)

            chunk_phase(U_A, FI_A, BI_A, AI_A, CH_A, True, 1)
            chunk_phase(U_M0, FI_M0, BI_M0, AI_M0, CH_M, False, 2, norm=1)
            pe.wait_ge(act_evac, FI_V2)
            pe.wait_ge(back_evac, BI_M1)
            ready(U_V2)
            for t in range(NT):
                pe.wait_ge(hT_done, 2 * HB + 2 * (t if t < 4 else NT - 1) + 2)
                n_item(DVE_EV, FI_V2 + t, V2_FIRST[t], 0, t, None if t < 6 else 5).then_inc(front_psum, 1)
                if 1 <= t <= 3:
                    transposes(2, NT - 4 + t)
            ready(U_V2 + 1)
            for t in range(NT):
                before = 3 if t >= 4 else 1 if t < 2 else None
                n_item(DVE_EV, FI_V2 + NT + t, t % 4, 1, t, before).then_inc(front_psum, 1)
            with pe.Fori(1, D // UC // 2) as i:
                n_units(DVE_EV, U_V2, FI_V2, i)

            with pe.Fori(0, D // UC) as i:
                for b in range(2):
                    ready(i * 2 + (U_QK + b))
                    for j in range(4):
                        t_item(DVE_EV, i * 8 + (FI_QK + 4 * b + j), j, b, j % 2, j // 2).then_inc(front_psum, 1)

            pe.wait_ge(dve_evac, FI_O - FI_V2)

            def scores(i, k):
                hb, _, zb, tb = tile_of(k)
                if tb == 0:
                    pe.wait_ge(qk_in[hb], (i + k // (2 * NT)) * (6 * 16) + 6 * 16)
                wait(pe, brk_done, i * (2 * NT) + (k - 1))
                s = (tb + 1) * P
                for c0 in range(0, s, HALF):
                    c1 = c0 + max(2 * P, min(HALF, s - c0))
                    for n in range(2):
                        mm = pe.matmul(z_ps[zb][:, c0:c1], q_st[hb][:, tb * P:(tb + 1) * P], k_st[hb][n][:, c0:c1],
                                       start=(n == 0), stop=(n == 1 and c1 < s))
                mm = pe.matmul(z_ps[zb][:, s - P:s], ident_bf[:], mask_bf[:], start=False, stop=True)
                mm.then_inc(z_done, 1)

            def to_keys(i, n, g):
                m, gi = pair(n), groups_before(n) + g
                if g == 0:
                    pe.wait_ge(a_done, i * (2 * NT) + (2 * n + 2))
                wait(pe, aT_lo, i * (2 * GH) + (gi - 1))
                for p in (2 * g, 2 * g + 1):
                    for e in range(2):
                        if p == 0 and e == 0:
                            continue
                        col = (1 - e) * P + (2 * m + 1 - p) * P
                        at_col = (p % 2) * 2 * P + e * P
                        mm = pe.transpose(psum[:, 4 + gi % 2, at_col:at_col + P], brk[m][e][:, col:col + P], ident[:])
                mm.then_inc(aT_psum, 1)

            def values(i, n, g):
                m, hb = pair(n), (n // QP) % 2
                if g == 0 and n % QP == 0:
                    pe.wait_ge(vh_in[hb], i * 16 + 16)
                if g == 0 and n % 2 == 0:
                    wait(pe, o_add, i * 4 + (n // 2 - 1))
                pe.wait_ge(aT_lo, i * (2 * GH) + (groups_before(n) + g + 1))
                for p in (2 * g, 2 * g + 1):
                    for s in range(2):
                        mm = pe.matmul(psum[:, 6 + m // 2, (m % 2) * 2 * P:(m % 2 + 1) * 2 * P],
                                       v_st[hb][:, 2 * m + 1 - p, :], aT[n % 2][s][:, p * 2 * P:(p + 1) * 2 * P],
                                       start=(p == 0 and s == 0), stop=(p == 2 * m + 1 and s == 1))
                mm.then_inc(av_done, 1)

            def att_step(i):
                first, last = isinstance(i, int) and i == 0, isinstance(i, int) and i == HEADS // 2 - 1
                if first:
                    for k in range(4):
                        scores(0, k)
                    pe.wait_ge(rows_set, 4)
                for n in range(2 * QP):
                    more = not (last and n >= 2 * QP - 2)
                    if more:
                        scores(i, 2 * n + 4)
                    here = pair(n) + 1
                    before = 0 if first and n == 0 else pair(n - 1) + 1
                    for g in range(max(here, before)):
                        if g < here:
                            to_keys(i, n, g)
                        if g < before:
                            if n:
                                values(i, n - 1, g)
                            else:
                                values(i - 1, 2 * QP - 1, g)
                        if more and g == 0:
                            scores(i, 2 * n + 5)
            iterate(pe, HEADS // 2, att_step)
            for g in range(pair(2 * QP - 1) + 1):
                values(HEADS // 2 - 1, 2 * QP - 1, g)

            pe.wait_ge(o_split, 2 * HEADS)
            pe.wait_ge(brk_done, HEADS * NT)
            for u in range(D // UC):
                ready(U_O + u)
                last = u == D // UC - 1
                for t in range(NT):
                    before = 3 if not last or t < 2 else 1
                    n_item(DVE_EV, FI_O + u * NT + t, t % (2 if last else 4), u % 2, t, before).then_inc(front_psum, 1)
                    if last and t >= 3:
                        if t == 3:
                            pe.wait_ge(dve_evac, FI_M1 - NT - FI_V2)
                        transposes(3, t - 3)
            pe.wait_ge(dve_evac, FI_M1 - FI_V2)
            chunk_phase(U_M1, FI_M1, BI_M1, AI_M1, CH_M, False, None, norm=3, gap=ACT_GAP)

        @block.scalar
        def _(act):
            def hi(n, b):
                act.wait_ge(unit_landed, n * 16 + 16)
                act.activation(wt[b][0][:], stage[:], ACT.Copy).then_inc(unit_hi, 1)

            def square_m(b, t):
                n = NT * (b - 1) + t
                if b == 3:
                    act.wait_ge(dve_evac, FI_M1 - FI_V2 - NT + t + 1)
                else:
                    act.wait_ge(back_evac, TAIL[b] + 2 * t + 2)
                wait(act, m_sq, n)
                act.wait_ge(x_sq, NT * b + max(0, t - 1) if b < 4 else NT * 4)
                act.activation(junk[:], acc[:, t, :], ACT.Square, accum_out=ss[:, 0, t:t + 1]).then_inc(m_sq, 1)
                act.wait_ge(m_sq, n + 1)
                act.activation(rt[:, 0, t:t + 1], ss[:, 0, t:t + 1], ACT.Sqrt, bias=eps[:, 0:1], scale=1.0 / D).then_inc(m_rt, 1)

            def square_x(b, t):
                n = NT * b + t
                if b:
                    x_new(act, b, t)
                else:
                    act.wait_ge(x_in[t % 4], 16 * (t // 4 + 1))
                wait(act, x_sq, n)
                if b:
                    act.wait_ge(m_sq, NT * (b - 1) + min(t + 2, NT))
                act.activation(junk[:], xt[t % 4][:], ACT.Square, accum_out=ss[:, 1, t:t + 1]).then_inc(x_sq, 1)
                act.wait_ge(x_sq, n + 1)
                act.activation(rt[:, 1, t:t + 1], ss[:, 1, t:t + 1], ACT.Sqrt, bias=eps[:, 0:1], scale=1.0 / D).then_inc(x_rt, 1)

            def take_hi(b, t):
                for q in range(2):
                    act.wait_ge(hT_psum, HB * b + 2 * t + q + 1)
                    act.activation(hT[0][:, 4 * q:4 * q + 4, t * P:(t + 1) * P],
                                   psum[:, hT_bank(b, t) + q, :].rearrange("p (k n) -> p k n", k=4),
                                   ACT.Copy).then_inc(front_hi, 1)

            def boundary(b, u_next=None, freed=None):
                for t in range(NT):
                    if b == 3 and t == 0:
                        act.wait_ge(front_psum, FI_O + 3 * NT)
                        hi(u_next, 0)
                    square_m(b, t)
                    if b < 4:
                        if t >= 3:
                            take_hi(b, t - 3)
                        if t:
                            square_x(b, t - 1)
                        if b in (1, 2) and t == NT - 2:
                            act.wait_ge(tail_first, b)
                            hi(u_next, 0)
                if b < 4:
                    square_x(b, NT - 1)
                    for t in range(NT - 3, NT):
                        take_hi(b, t)
                    act.wait_ge(*freed)
                    hi(u_next + 1, 1)

            act.wait_ge(eps_set, 1)
            for t in range(NT + 1):
                if t < NT:
                    square_x(0, t)
                if t:
                    take_hi(0, t - 1)
                if t == 2:
                    hi(U_V, 0)
            hi(U_V + 1, 1)

            def v_store(u, b):
                act.dma_start(v_dram[bass.ds(u, 1)].rearrange("o p f -> (o p) f"),
                              vring[:, b].rearrange("p t f -> p (t f)")).then_inc(v_out[b], 16)

            for t in range(NT):
                act.wait_ge(front_psum, FI_V + t + (2 if t % 2 == 0 else 1))
                act.activation(vring[:, 0, t, :], psum[:, 4 + t // 2, (t % 2) * UC:(t % 2 + 1) * UC],
                               ACT.Gelu).then_inc(act_evac, 1)
            hi(U_V + 2, 0)
            act.wait_ge(act_evac, FI_V + NT)
            v_store(0, 0)
            for t in range(NT):
                act.wait_ge(front_psum, FI_V + NT + t + 1)
                act.activation(vring[:, 1, t, :], psum[:, t % 4, 0:UC], ACT.Gelu).then_inc(act_evac, 1)
                if t == 3:
                    for q in range(2):
                        act.wait_ge(back_psum, q + 1)
                        act.activation(wsT[:, 4 * q:4 * q + 4, 0, :], psum[:, 4 + q, :].rearrange("p (g n) -> p g n", g=4),
                                       ACT.Copy).then_inc(ws_hi, 1)
            hi(U_V + 3, 1)
            act.wait_ge(act_evac, FI_V + 2 * NT)
            v_store(1, 1)

            def v_units(i, last=False):
                for b in range(2):
                    act.wait_ge(v_out[b], i * 16)
                    act.wait_ge(v_stats, i * (2 * NT) + (b - 1) * NT)
                    for t in range(NT):
                        act.wait_ge(front_psum, i * (2 * NT) + (FI_V + b * NT + t + 1))
                        act.activation(vring[:, b, t, :], psum[:, t % 4, 0:UC], ACT.Gelu).then_inc(act_evac, 1)
                    if not (last and b):
                        hi(i * 2 + (U_V + b + 2), b)
                    act.wait_ge(act_evac, i * (2 * NT) + (FI_V + (b + 1) * NT))
                    v_store(2 * i + b, b)

            with act.Fori(1, AW // UC // 2 - 1) as i:
                v_units(i)
            v_units(AW // UC // 2 - 1, last=True)
            act.wait_ge(v_norm, NT)
            act.activation(v_rt[:], mv[:, :, 1], ACT.Sqrt, bias=eps[:, 0:1], scale=1.0).then_inc(v_sqrt, 1)

            hi(U_A + 1, 1)

            def gate_chunk(c, ab):
                if not (isinstance(c, int) and c == 0):
                    act.wait_ge(back_psum, s_end(c - 2, BI_A, 20, 8))
                    hi(c * 2 + U_A, 0)
                wait(act, vn_nat, c + 1)
                if not (isinstance(c, int) and c == 0):
                    act.wait_ge(back_psum, mix_item(c - 1) + 4)
                act.activation(vn[0][:], vst[:], ACT.Copy).then_inc(vn_hi, 1)

                def gelu(j):
                    act.wait_ge(front_psum, c * 4 + (FI_A + j + 1))
                    wait(act, ch_lo, c * 4 + (j - 3))
                    act.activation(ut[:, j, :], psum[:, j, :], ACT.Gelu).then_inc(act_evac, 1)

                def gated_hi(j):
                    act.wait_ge(back_evac, mix_item(c) + (j + 1))
                    act.wait_ge(back_psum, s_end(c - 2, BI_A, 20, 8))
                    act.activation(a_buf[ab][0][:, j % 2, (j // 2) * HALF:(j // 2 + 1) * HALF], ut[:, j, :],
                                   ACT.Copy).then_inc(ch_hi, 1)

                gelu(0)
                gelu(1)
                gated_hi(0)
                gelu(2)
                gated_hi(1)
                last = isinstance(c, int) and c == CH_A - 1
                if last:
                    act.wait_ge(front_psum, FI_A + 4 * CH_A)
                    hi(c * 2 + (U_A + 1), 1)
                gelu(3)
                gated_hi(2)
                if not last and not (isinstance(c, int) and c == 0):
                    hi(c * 2 + (U_A + 1), 1)
                gated_hi(3)

            def gate_step(i):
                if isinstance(i, int) and i == 0:
                    gate_chunk(0, 0)
                gate_chunk(2 * i + 1, 1)
                if not (isinstance(i, int) and i == CH_A // 2 - 1):
                    gate_chunk(2 * i + 2, 0)
            iterate(act, CH_A // 2, gate_step)
            boundary(1, U_M0, (back_psum, BI_M0))

            def mlp(u0, fi0, ai0, bi0, gap=0):
                def chunk(c, ab):
                    if not (isinstance(c, int) and c == 0):
                        act.wait_ge(back_psum, s_end(c - 2, bi0, 16, 0))
                        hi(c * 2 + u0, 0)
                    for j in range(4):
                        act.wait_ge(front_psum, c * 4 + (fi0 + j + 1))
                        if j == 3 and not (isinstance(c, int) and c == 0):
                            hi(c * 2 + (u0 + 1), 1)
                        wait(act, ch_lo, c * 4 + (ai0 + j - 1))
                        act.activation(relu[j % 2][:], psum[:, j, :], ACT.Relu).then_inc(act_evac, 1)
                        act.wait_ge(act_evac, c * 4 + (fi0 - gap + j + 1))
                        act.wait_ge(back_psum, s_end(c - 2, bi0, 16, 0))
                        act.activation(a_buf[ab][0][:, j % 2, (j // 2) * HALF:(j // 2 + 1) * HALF], relu[j % 2][:],
                                       ACT.Square).then_inc(ch_hi, 1)

                def step(i):
                    if isinstance(i, int) and i == 0:
                        chunk(0, 0)
                    chunk(2 * i + 1, 1)
                    if not (isinstance(i, int) and i == CH_M // 2 - 1):
                        chunk(2 * i + 2, 0)
                iterate(act, CH_M // 2, step)

            mlp(U_M0, FI_M0, AI_M0, BI_M0)
            boundary(2, U_V2, (back_psum, BI_M1))

            for u in range(D // UC):
                b = u % 2
                if u >= 2:
                    act.wait_ge(v2_out[b], 64 * (u // 2))
                for t in range(NT):
                    act.wait_ge(front_psum, FI_V2 + u * NT + t + 1)
                    act.activation(v2ring[b][:, :, t, 0, :],
                                   psum[:, t % 4 if u else V2_FIRST[t], 0:UC].rearrange("p (h d) -> p h d", h=4),
                                   ACT.Copy).then_inc(front_hi, 1)
                hi(U_V2 + u + 2, b)
                act.wait_ge(dve_evac, (u + 1) * NT)
                for j in range(4):
                    act.dma_start(v2_dram[4 * u + j].bitcast(F32),
                                  v2ring[b][:, j].rearrange("p t s d -> p (t s d)").bitcast(F32)).then_inc(v2_out[b], 16)

            def qk_step(i):
                for b in range(2):
                    if not (isinstance(i, int) and i == 0):
                        act.wait_ge(qk_out[b], i * 32)
                    for j in range(4):
                        act.wait_ge(front_psum, i * 8 + (FI_QK + 4 * b + j + 1))
                        act.activation(a_buf[b][0][:, j % 2, (j // 2) * HALF:(j // 2 + 1) * HALF], psum[:, j, :],
                                       ACT.Copy).then_inc(front_hi, 1)
                    hi(i * 2 + (U_QK + b + 2), b)
                    act.wait_ge(dve_evac, i * 8 + (FI_QK - FI_V2 + 4 * b + 4))
                    for s in range(2):
                        act.dma_start(qk_dram[s].rearrange("(u p) n -> p u n", p=P)[:, bass.ds(4 * i + 2 * b, 2), :].bitcast(F32),
                                      a_buf[b][s][:].bitcast(F32)).then_inc(qk_out[b], 16)
            qk_step(0)
            with act.Fori(1, D // UC) as i:
                qk_step(i)
            act.wait_ge(qk_out[0], 32 * (2 * D // UC) // 2)
            act.wait_ge(x_out, 16 * NT * 2)

            def keep_tile(i, k):
                _, m, e, tb = tile_of(k)
                act.wait_ge(z_done, i * (2 * NT) + (k + 1))
                wait(act, a_done, i * (2 * NT) + (k - NT + 1))
                act.activation(stick[m][e][:, (1 - e) * P:(2 * m + 2) * P], z_ps[e][:, 0:(tb + 1) * P],
                               ACT.Sigmoid, scale=-SCALE).then_inc(keep_done, 1)

            def break_tile(i, k):
                _, m, e, tb = tile_of(k)
                wait(act, aT_psum, i * (2 * GH) + groups_before(k // 2 - QP + 1))
                act.activation(brk[m][e][:, (1 - e) * P:(2 * m + 2) * P], z_ps[e][:, 0:(tb + 1) * P],
                               ACT.Sigmoid, scale=SCALE).then_inc(brk_done, 1)

            def keys_hi(i, n, g):
                gi, c0 = groups_before(n) + g, P if g == 0 else 0
                act.wait_ge(aT_psum, i * (2 * GH) + (gi + 1))
                wait(act, av_done, i * (2 * GH) + groups_before(n - 1))
                act.activation(aT[n % 2][0][:, g * HALF + c0:(g + 1) * HALF], psum[:, 4 + gi % 2, c0:HALF],
                               ACT.Copy).then_inc(aT_hi, 1)

            def out_low(i, r):
                act.wait_ge(av_done, i * (2 * GH) + groups_before(2 * r + 2))
                wait(act, o_add, i * 4 + (r - 1))
                act.activation(o_low[:, r % 2, :], psum[HD:P, 6 + r % 2, :], ACT.Copy).then_inc(o_lo, 1)

            def out_hi(i, r):
                h2, g = r // 2, r % 2
                act.wait_ge(o_add, i * 4 + (r + 1))
                act.wait_ge(o_add, 1)
                act.activation(hT[0][h2 * HD:(h2 + 1) * HD, bass.ds(i, 1), g * HALF:(g + 1) * HALF],
                               o_sum[h2 * HD:(h2 + 1) * HD, g:g + 1, :], ACT.Copy).then_inc(o_hi, 1)

            def att_step(i):
                first, last = isinstance(i, int) and i == 0, isinstance(i, int) and i == HEADS // 2 - 1
                if first:
                    for k in range(4):
                        keep_tile(0, k)
                        break_tile(0, k)
                    act.wait_ge(qk_out[1], 32 * (2 * D // UC) // 2)
                for n in range(2 * QP):
                    out = None if n % 2 == 0 or (first and n == 1) else (i, n // 2 - 1) if n > 1 else (i - 1, 3)
                    for g in range(4):
                        if not (last and n >= 2 * QP - 2):
                            (keep_tile if g % 2 == 0 else break_tile)(i, 2 * n + 4 + g // 2)
                        if g <= pair(n):
                            keys_hi(i, n, g)
                        if out and g == 1:
                            out_low(*out)
                    if out:
                        out_hi(*out)
            iterate(act, HEADS // 2, att_step)
            out_low(HEADS // 2 - 1, 3)
            out_hi(HEADS // 2 - 1, 3)

            for u in range(2, D // UC):
                act.wait_ge(front_psum, FI_O + (u - 1) * NT)
                hi(U_O + u, u % 2)
            boundary(3, U_M1, (front_psum, FI_M1))
            mlp(U_M1, FI_M1, AI_M1, BI_M1, ACT_GAP)
            boundary(4)

        @block.vector
        def _(dve):
            def post_norm(b, t):
                n = NT * (b - 1) + t
                before = post_steps(b, t - 1)
                dve.wait_ge(m_rt, n + 1)
                dve.reciprocal(rstd[:, 0, t:t + 1], rt[:, 0, t:t + 1]).then_inc(post, 1)
                dve.wait_ge(post, before + 1)
                if t == 0:
                    dve.wait_ge(g_in, 16 * (1 + 2 * (b - 1) + 2) if b < 4 else 16 * 8)
                dve.scalar_tensor_tensor(acc[:, t, :], acc[:, t, :], rstd[:, 0, t:t + 1], gpost[:], ALU.mult, ALU.mult).then_inc(post, 1)
                if t >= 6:
                    dve.wait_ge(post, before + 2)
                    dve.wait_ge(x_in[t % 4], 16 * (2 * b + t // 4 + 1))
                    dve.tensor_tensor(xt[t % 4][:], acc[:, t, :], xt[t % 4][:], ALU.add).then_inc(post, 1)

            def pre_norm(b, t):
                n = NT * b + t
                dve.wait_ge(x_rt, n + 1)
                dve.reciprocal(rstd[:, 1, t:t + 1], rt[:, 1, t:t + 1]).then_inc(pre, 1)
                dve.wait_ge(pre, 2 * n + 1)
                if b == 0 and t == 0:
                    dve.wait_ge(g_in, 16)
                wait(dve, hT_psum, HB * b + 2 * t - 2)
                dve.scalar_tensor_tensor(h_nat[t % 2][:], xt[t % 4][:], rstd[:, 1, t:t + 1], gpre[:], ALU.mult, ALU.mult).then_inc(pre, 1)

            hi_count = [0]

            def take_lo(b, t):
                for q in range(2):
                    hi_count[0] += 1
                    dve.wait_ge(front_hi, hi_count[0])
                    dst = slice(t * P, (t + 1) * P)
                    dve.tensor_tensor(hT[1][:, 4 * q:4 * q + 4, dst], psum[:, hT_bank(b, t) + q, :].rearrange("p (k n) -> p k n", k=4),
                                      hT[0][:, 4 * q:4 * q + 4, dst].bitcast(F32), ALU.subtract).then_inc(hT_done, 1)

            def boundary(b, finish):
                for t in range(NT):
                    finish(t)
                    if b < 4 and t >= 2:
                        pre_norm(b, t - 2)
                    post_norm(b, t)
                    if b < 4 and t >= 3:
                        take_lo(b, t - 3)
                if b < 4:
                    pre_norm(b, NT - 2)
                    take_lo(b, NT - 3)
                    pre_norm(b, NT - 1)
                    take_lo(b, NT - 2)
                    take_lo(b, NT - 1)

            for t in range(NT + 1):
                if t < NT:
                    pre_norm(0, t)
                if t:
                    take_lo(0, t - 1)

            for q in range(2):
                dve.wait_ge(ws_hi, q + 1)
                dve.tensor_tensor(wsT[:, 4 * q:4 * q + 4, 1, :], psum[:, 4 + q, :].rearrange("p (g n) -> p g n", g=4),
                                  wsT[:, 4 * q:4 * q + 4, 0, :].bitcast(F32), ALU.subtract).then_inc(back_evac, 1)
            for q in range(2):
                dve.wait_ge(back_psum, q + 3)
                dve.tensor_copy(rs_bc[:, q * HALF:(q + 1) * HALF], psum[:, 6 + q, :]).then_inc(back_evac, 1)

            with dve.Fori(0, AW // UC // 2) as i:
                for b in range(2):
                    for t in range(NT):
                        dve.wait_ge(act_evac, i * (2 * NT) + (FI_V + b * NT + t + 1))
                        dve.wait_ge(act_evac, FI_V + 1)
                        dve.bn_stats(stats[:, t, bass.ds(2 * i + b, 1), :], vring[:, b, t, :]).then_inc(v_stats, 1)
            dve.wait_ge(v_stats, NT * AW // UC)
            for t in range(NT):
                dve.bn_aggr(mv[:, t, :], stats[:, t].rearrange("p u s -> p (u s)")).then_inc(v_norm, 1)
            dve.wait_ge(v_sqrt, 1)
            dve.reciprocal(v_rs[:], v_rt[:]).then_inc(v_norm, 1)
            dve.wait_ge(v_norm, NT + 1)
            dve.wait_ge(vecs, 48)
            for b in range(2):
                dve.wait_ge(v_out[b], 16 * AW // UC // 2)

            def accumulate(c_first, bi, j, per):
                dve.wait_ge(back_psum, bi + 1)
                dst = acc[:, j // 2, (j % 2) * HALF:(j % 2 + 1) * HALF]
                src = psum[:, 4 + j % 4, :]
                if c_first:
                    return dve.tensor_copy(dst, src)
                dve.wait_ge(back_evac, bi - (per - 1))
                return dve.tensor_tensor(dst, src, dst, ALU.add)

            def gate_chunk(c, ab):
                dve.wait_ge(v_in, c * 16 + 16)
                for t in range(NT):
                    ins = dve.tensor_scalar(vst[:, t, :], vst[:, t, :], mv[:, t, 0:1], v_rs[:, t:t + 1],
                                            ALU.subtract, ALU.mult)
                ins.then_inc(vn_nat, 1)
                wait(dve, gate, c * 8)
                for f in range(2):
                    dve.scalar_tensor_tensor(bb[:, f, :], rs_bc[:, bass.ds(c * P, P)], vb_c[:, bass.ds(c * 2 + f, 1)],
                                             bs_bc[:, bass.ds(c * P, P)], ALU.mult, ALU.add).then_inc(bb_set, 1)
                dve.wait_ge(vn_hi, c + 1)
                dve.tensor_tensor(vn[1][:], vst[:], vn[0][:].bitcast(F32), ALU.subtract).then_inc(vn_lo, 1)
                dve.wait_ge(bb_set, c * 2 + 2)

                def gated_lo(j):
                    dve.wait_ge(ch_hi, c * 4 + (j + 1))
                    dst = (slice(None), j % 2, slice((j // 2) * HALF, (j // 2 + 1) * HALF))
                    dve.tensor_tensor(a_buf[ab][1][dst], ut[:, j, :], a_buf[ab][0][dst].bitcast(F32),
                                      ALU.subtract).then_inc(ch_lo, 1)

                for j in range(4):
                    f = j % 2
                    bi = mix_item(c) + j
                    dve.wait_ge(back_psum, bi + 1)
                    dve.wait_ge(act_evac, c * 4 + (FI_A + j + 1))
                    mixed = psum[:, 4 + 2 * f:6 + 2 * f, :].rearrange("p a (t s n) -> p (a t) s n", t=2, s=2)
                    u = ut[:, j, :].rearrange("p (t n) -> p t n", t=4)
                    v_gain = vg_c[:, bass.ds(c * 2 + f, 1)]
                    dve.scalar_tensor_tensor(mix_lo[:], mixed[:, :, 1], v_gain,
                                             bb[:, f:f + 1, :].to_broadcast([P, 4, P]), ALU.mult, ALU.add).then_inc(gate, 1)
                    dve.wait_ge(gate, c * 8 + (2 * j + 1))
                    dve.scalar_tensor_tensor(mixed[:, :, 0], mixed[:, :, 0], v_gain, mix_lo[:],
                                             ALU.mult, ALU.add).then_inc(gate, 1)
                    dve.wait_ge(gate, c * 8 + (2 * j + 2))
                    dve.tensor_tensor(u, mixed[:, :, 0], u, ALU.mult).then_inc(back_evac, 1)
                    if j:
                        gated_lo(j - 1)
                gated_lo(3)

            def s_part(c, bi0, per, extra, copy):
                for j in range(16):
                    accumulate(copy, c * per + (bi0 + extra + j), j, per).then_inc(back_evac, 1)

            def gate_step(i):
                first = isinstance(i, int) and i == 0
                if first:
                    gate_chunk(0, 0)
                gate_chunk(2 * i + 1, 1)
                if isinstance(i, int) and i == CH_A // 2 - 1:
                    return
                s_part(2 * i, BI_A, 20, 8, first)
                gate_chunk(2 * i + 2, 0)
                s_part(2 * i + 1, BI_A, 20, 8, False)
            iterate(dve, CH_A // 2, gate_step)

            def finish_tail(b):
                bi, per = TAIL[b], 20 if b == 1 else 16

                def finish(t):
                    for n2 in range(2):
                        ins = accumulate(False, bi + 2 * t + n2, 2 * t + n2, per)
                        ins.then_inc(back_evac, 1)
                return finish

            boundary(1, finish_tail(1))

            def mlp(ai0, bi0, r0):
                def chunk(c, ab):
                    for j in range(4):
                        dst = (slice(None), j % 2, slice((j // 2) * HALF, (j // 2 + 1) * HALF))
                        dve.wait_ge(ch_hi, c * 4 + (ai0 + j + 1))
                        dve.tensor_tensor(relu[j % 2][:], relu[j % 2][:], relu[j % 2][:], ALU.mult).then_inc(relu_sq, 1)
                        dve.wait_ge(relu_sq, c * 4 + (r0 + j + 1))
                        dve.tensor_tensor(a_buf[ab][1][dst], relu[j % 2][:], a_buf[ab][0][dst].bitcast(F32),
                                          ALU.subtract).then_inc(ch_lo, 1)

                def step(i):
                    first = isinstance(i, int) and i == 0
                    if first:
                        chunk(0, 0)
                    chunk(2 * i + 1, 1)
                    if isinstance(i, int) and i == CH_M // 2 - 1:
                        return
                    s_part(2 * i, bi0, 16, 0, first)
                    chunk(2 * i + 2, 0)
                    s_part(2 * i + 1, bi0, 16, 0, False)
                iterate(dve, CH_M // 2, step)

            mlp(AI_M0, BI_M0, 0)
            boundary(2, finish_tail(2))

            for u in range(D // UC):
                b = u % 2
                for t in range(NT):
                    hi_count[0] += 1
                    dve.wait_ge(front_hi, hi_count[0])
                    dve.tensor_tensor(v2ring[b][:, :, t, 1, :],
                                      psum[:, t % 4 if u else V2_FIRST[t], 0:UC].rearrange("p (h d) -> p h d", h=4),
                                      v2ring[b][:, :, t, 0, :].bitcast(F32), ALU.subtract).then_inc(dve_evac, 1)
            with dve.Fori(0, D // UC) as i:
                for b in range(2):
                    for j in range(4):
                        dst = (slice(None), j % 2, slice((j // 2) * HALF, (j // 2 + 1) * HALF))
                        dve.wait_ge(front_hi, i * 8 + (hi_count[0] + 4 * b + j + 1))
                        ins = dve.tensor_tensor(a_buf[b][1][dst], psum[:, j, :], a_buf[b][0][dst].bitcast(F32), ALU.subtract)
                        ins.then_inc(dve_evac, 1)
            hi_count[0] += 4 * 2 * D // UC

            dve.wait_ge(x_out, 16 * NT * 2)
            for b in range(2):
                for s in range(2):
                    dve.memset(aT[b][s][:, 0:P].bitcast(F32), 0.0).then_inc(rows_set, 1)

            def ones_column(m):
                for e in range(2):
                    dve.memset(stick[m][e][:, (2 * m + 2) * P:(2 * m + 2) * P + 1], 1.0).then_inc(rows_set, 1)

            dve.wait_ge(qk_out[0], 32 * (2 * D // UC) // 2)
            for m in range(QP - 1):
                ones_column(m)
            dve.wait_ge(rows_set, 4 + 2 * (QP - 1))

            def sticks(i, k):
                _, m, e, tb = tile_of(k)
                dve.wait_ge(keep_done, i * (2 * NT) + (k + 1))
                row = stick[m][e][:, (1 - e) * P:(2 * m + 2) * P][:, ::-1]
                dve.tensor_tensor_scan(row, row, row, 1.0, ALU.mult, ALU.bypass).then_inc(stick_done, 1)

            def keys_lo(i, n, g):
                gi, c0 = groups_before(n) + g, P if g == 0 else 0
                dst = (slice(None), slice(g * HALF + c0, (g + 1) * HALF))
                dve.wait_ge(aT_hi, i * (2 * GH) + (gi + 1))
                dve.tensor_tensor(aT[n % 2][1][dst], psum[:, 4 + gi % 2, c0:HALF],
                                  aT[n % 2][0][dst].bitcast(F32), ALU.subtract).then_inc(aT_lo, 1)

            def out_sum(i, r):
                h2, g = r // 2, r % 2
                half = slice(h2 * HD, (h2 + 1) * HD)
                dve.wait_ge(o_lo, i * 4 + (r + 1))
                wait(dve, o_split, i * 4 + (r - 1))
                dve.tensor_tensor(o_sum[half, g, :], psum[0:HD, 6 + g, :], o_low[:, g, :], ALU.add).then_inc(o_add, 1)

            def out_lo(i, r):
                h2, g = r // 2, r % 2
                half = slice(h2 * HD, (h2 + 1) * HD)
                dve.wait_ge(o_hi, i * 4 + (r + 1))
                dst = (half, bass.ds(i, 1), slice(g * HALF, (g + 1) * HALF))
                dve.tensor_tensor(hT[1][dst], o_sum[half, g:g + 1, :], hT[0][dst].bitcast(F32),
                                  ALU.subtract).then_inc(o_split, 1)

            def att_step(i):
                first, last = isinstance(i, int) and i == 0, isinstance(i, int) and i == HEADS // 2 - 1
                if first:
                    for k in range(4):
                        sticks(0, k)
                    dve.wait_ge(qk_out[1], 32 * (2 * D // UC) // 2)
                    ones_column(QP - 1)
                    dve.wait_ge(rows_set, 4 + 2 * QP)
                for n in range(2 * QP):
                    more = not (last and n >= 2 * QP - 2)
                    out = None if n % 2 == 0 or (first and n == 1) else (i, n // 2 - 1) if n > 1 else (i - 1, 3)
                    for g in range(4):
                        if more and g % 2 == 0:
                            sticks(i, 2 * n + 4 + g // 2)
                        if g <= pair(n):
                            keys_lo(i, n, g)
                        if out and g == 1:
                            out_sum(*out)
                    if out:
                        out_lo(*out)
            iterate(dve, HEADS // 2, att_step)
            out_sum(HEADS // 2 - 1, 3)
            out_lo(HEADS // 2 - 1, 3)

            def o_part(u, t):
                bank = t % (4 if u < D // UC - 1 else 2)
                dve.wait_ge(front_psum, FI_O + u * NT + t + 1)
                if u == 0 and t == 0:
                    dve.wait_ge(av_done, GH * HEADS)
                return dve.tensor_copy(acc[:, t, u * UC:(u + 1) * UC], psum[:, bank, 0:UC])

            for u in range(D // UC - 1):
                for t in range(NT):
                    o_part(u, t).then_inc(dve_evac, 1)

            def o_finish(t):
                o_part(D // UC - 1, t).then_inc(dve_evac, 1)
            boundary(3, o_finish)
            mlp(AI_M1, BI_M1, 4 * CH_M)
            boundary(4, finish_tail(4))


TAIL = {1: BI_A + 20 * (CH_A - 2) + 8, 2: BI_M0 + 16 * (CH_M - 2), 4: BI_M1 + 16 * (CH_M - 2)}


INPUTS = ["x", "norm_mix_pre", "norm_mix_post", "norm_ffn_pre", "norm_ffn_post", "a_w_in", "a_v_g", "a_v_b",
          "a_w_s", "a_b_s", "a_w_out", "b_w_qkv", "b_w_out", "mlp_w1", "mlp_w2"]


def kernel(**inputs):
    import numpy as np
    import concourse.bacc as bacc
    from concourse.bass_utils import run_bass_kernel_spmd

    nc = bacc.Bacc("TRN2", target_bir_lowering=False, num_devices=1, dynamic_dma_scratch_size=1024)
    arrays, ap = {}, {}
    for name in INPUTS:
        a = np.ascontiguousarray(inputs[name])
        arrays[name + "_in"] = a
        ap[name] = nc.dram_tensor(name + "_in", a.shape, F32, kind="ExternalInput").ap()
    y = nc.dram_tensor("y_out", (TOK, D), F32, kind="ExternalOutput").ap()
    build(nc, ap["x"][0], ap["norm_mix_pre"], ap["norm_mix_post"], ap["norm_ffn_pre"], ap["norm_ffn_post"],
          ap["a_w_in"][0], ap["a_v_g"], ap["a_v_b"], ap["a_w_s"][0], ap["a_b_s"][0], ap["a_w_out"][0],
          ap["b_w_qkv"][0], ap["b_w_out"][0], ap["mlp_w1"], ap["mlp_w2"], y)
    r = run_bass_kernel_spmd(nc, [arrays], core_ids=[0])
    return r.results[0]["y_out"].reshape(1, TOK, D)
```
